# Optimizing a Trainium2 kernel written in Bass

```python
import math
import jax, jax.numpy as jnp
from jax import lax
import numpy as np

'''Hybrid autoregressive decoder trunk, DEPTH consecutive layers, with 16 learned meta tokens
prepended before the first layer and dropped at the end.

Even layers: pre-RMSNorm -> ONE combined input projection whose columns are split into
  (A) a causal Conformer convolution group (GLU -> depthwise conv w=31 -> LayerNorm -> swish), 512 channels
  (B) a stick-breaking attention group (8 heads x 64, QK RMS-norm, no positional encoding, strictly causal)
  -> outputs concatenated -> ONE output projection -> residual add;
  then pre-RMSNorm dense SwiGLU -> residual add.
Odd layers: pre-RMSNorm -> Griffin recurrent block (gelu gate branch; width-4 causal depthwise conv;
  RG-LRU with block-diagonal gates, 16 blocks) -> output projection -> residual add;
  then pre-RMSNorm top-2-of-8 SwiGLU experts -> residual add.

Inputs: x (BATCH, SEQ, D_MODEL) float32 plus parameters (stacked over even / odd layers).
Output: (BATCH, SEQ, D_MODEL).
'''

D_MODEL = 1024
BATCH = 1
SEQ = 256
DEPTH = 2

N_META = 16
N_EVEN = (DEPTH + 1) // 2
N_ODD = DEPTH // 2
EPS = 1e-6

CONV_CH = D_MODEL // 2
CONV_WIDTH = 31
SB_HEADS = 8
SB_HEAD_DIM = 64
SB_WIDTH = SB_HEADS * SB_HEAD_DIM
Q_BLOCK = 128
EVEN_IN = 2 * CONV_CH + 3 * SB_WIDTH
EVEN_MIX = CONV_CH + SB_WIDTH

LRU_WIDTH = 1408
LRU_BLOCKS = 16
LRU_BLOCK_DIM = LRU_WIDTH // LRU_BLOCKS
LRU_CONV_WIDTH = 4
LRU_C = 8.0

D_FF = 2688
N_EXPERTS = 8
TOP_K = 2
D_FF_EXPERT = 3584

kernel_name = 'hybrid_conv_stickbreak_rglru_moe'

def rms_norm(x, g):
    xf = x.astype(jnp.float32)
    y = xf * lax.rsqrt(jnp.mean(xf * xf, axis=-1, keepdims=True) + EPS)
    return (y * g.astype(jnp.float32)).astype(x.dtype)

def layer_norm(x, g, b):
    xf = x.astype(jnp.float32)
    mu = jnp.mean(xf, axis=-1, keepdims=True)
    xc = xf - mu
    var = jnp.mean(xc * xc, axis=-1, keepdims=True)
    y = xc * lax.rsqrt(var + EPS) * g.astype(jnp.float32) + b.astype(jnp.float32)
    return y.astype(x.dtype)

def causal_depthwise_conv(x, w, b):
    k_w = w.shape[0]
    c = x.shape[-1]
    y = lax.conv_general_dilated(
        x, w[:, None, :].astype(x.dtype), window_strides=(1,), padding=[(k_w - 1, 0)],
        dimension_numbers=('NWC', 'WIO', 'NWC'), feature_group_count=c)
    return y + b.astype(x.dtype)

def stick_breaking_block(q_blk, q_pos, k, v):
    z = jnp.einsum('bhqd,bhkd->bhqk', q_blk, k,
                   preferred_element_type=jnp.float32) / math.sqrt(SB_HEAD_DIM)
    k_pos = jnp.arange(k.shape[2])
    mask = k_pos[None, :] < q_pos[:, None]
    log_not = jnp.where(mask, jax.nn.log_sigmoid(-z), 0.0)
    rev = lax.cumsum(log_not, axis=3, reverse=True)
    later = jnp.concatenate([rev[..., 1:], jnp.zeros_like(rev[..., :1])], axis=-1)
    w = jnp.where(mask, jnp.exp(jax.nn.log_sigmoid(z) + later), 0.0)
    return jnp.einsum('bhqk,bhkd->bhqd', w.astype(v.dtype), v)

def stick_breaking(q, k, v):
    b, h, t, dh = q.shape
    s = t - N_META
    nb = s // Q_BLOCK
    meta_out = stick_breaking_block(q[:, :, :N_META], jnp.arange(N_META),
                                    k[:, :, :N_META], v[:, :, :N_META])
    q_real = q[:, :, N_META:].reshape(b, h, nb, Q_BLOCK, dh).transpose(2, 0, 1, 3, 4)
    pos = (N_META + jnp.arange(s)).reshape(nb, Q_BLOCK)
    out = lax.map(lambda a: stick_breaking_block(a[0], a[1], k, v), (q_real, pos))
    out = out.transpose(1, 2, 0, 3, 4).reshape(b, h, s, dh)
    return jnp.concatenate([meta_out, out], axis=2)

def conv_sb_mixer(x, norm_g, w_in, conv_w, conv_b, conv_ln_g, conv_ln_b, q_norm_g, k_norm_g, w_out):
    b, t, _ = x.shape
    hcat = rms_norm(x, norm_g) @ w_in
    conv_a, conv_gate, q, k, v = jnp.split(
        hcat, [CONV_CH, 2 * CONV_CH, 2 * CONV_CH + SB_WIDTH, 2 * CONV_CH + 2 * SB_WIDTH], axis=-1)
    u = conv_a * jax.nn.sigmoid(conv_gate)
    u = causal_depthwise_conv(u, conv_w, conv_b)
    u = jax.nn.silu(layer_norm(u, conv_ln_g, conv_ln_b))
    def heads(a):
        return a.reshape(b, t, SB_HEADS, SB_HEAD_DIM).transpose(0, 2, 1, 3)
    qh = rms_norm(heads(q), q_norm_g)
    kh = rms_norm(heads(k), k_norm_g)
    o = stick_breaking(qh, kh, heads(v)).transpose(0, 2, 1, 3).reshape(b, t, SB_WIDTH)
    return jnp.concatenate([u, o.astype(u.dtype)], axis=-1) @ w_out

def rglru_mixer(x, norm_g, w_in, conv_w, conv_b, gate_r_w, gate_r_b, gate_i_w, gate_i_b, lru_lambda, w_out):
    b, t, _ = x.shape
    hcat = rms_norm(x, norm_g) @ w_in
    gate, xb = jnp.split(hcat, 2, axis=-1)
    gate = jax.nn.gelu(gate, approximate=True)
    xb = causal_depthwise_conv(xb, conv_w, conv_b)
    xblk = xb.reshape(b, t, LRU_BLOCKS, LRU_BLOCK_DIM)
    r = jax.nn.sigmoid(jnp.einsum('btni,nij->btnj', xblk, gate_r_w).reshape(b, t, LRU_WIDTH) + gate_r_b)
    i = jax.nn.sigmoid(jnp.einsum('btni,nij->btnj', xblk, gate_i_w).reshape(b, t, LRU_WIDTH) + gate_i_b)
    log_a = -LRU_C * r.astype(jnp.float32) * jax.nn.softplus(-lru_lambda.astype(jnp.float32))
    a = jnp.exp(log_a)
    bx = jnp.sqrt(-jnp.expm1(2.0 * log_a)) * (i * xb).astype(jnp.float32)

    def step(hstate, ab):
        a_t, b_t = ab
        hstate = a_t * hstate + b_t
        return hstate, hstate

    _, hs = lax.scan(step, jnp.zeros((b, LRU_WIDTH), jnp.float32),
                     (a.transpose(1, 0, 2), bx.transpose(1, 0, 2)))
    y = hs.transpose(1, 0, 2).astype(x.dtype)
    return (gate * y) @ w_out

def swiglu(x, w_gate, w_up, w_down):
    return (jax.nn.silu(x @ w_gate) * (x @ w_up)) @ w_down

def moe_swiglu(x, router_w, w_gate, w_up, w_down):
    b, t, d = x.shape
    xf = x.reshape(b * t, d)
    logits = (xf @ router_w).astype(jnp.float32)
    top_vals, top_idx = lax.top_k(logits, TOP_K)
    top_w = jax.nn.softmax(top_vals, axis=-1)
    gates = jnp.sum(jax.nn.one_hot(top_idx, N_EXPERTS, dtype=jnp.float32) * top_w[..., None], axis=1)
    y = jnp.zeros_like(xf)
    for e in range(N_EXPERTS):
        y = y + gates[:, e:e + 1].astype(x.dtype) * swiglu(xf, w_gate[e], w_up[e], w_down[e])
    return y.reshape(b, t, d)

def setup_inputs(seed: int = 0) -> dict:
    key = jax.random.key(seed)
    ks = list(jax.random.split(key, 40))
    D = D_MODEL
    PE, PO = N_EVEN, N_ODD

    def nrm(k, shape, scale):
        return scale * jax.random.normal(k, shape, jnp.float32)

    def gain(k, shape):
        return 1.0 + 0.05 * jax.random.normal(k, shape, jnp.float32)

    u = jax.random.uniform(ks[26], (PO, LRU_WIDTH), jnp.float32, 0.9, 0.999)
    p = u ** (1.0 / LRU_C)
    lru_lambda = jnp.log(p) - jnp.log1p(-p)

    return {
        'x': nrm(ks[0], (BATCH, SEQ, D), 1.0),
        'meta_tokens': nrm(ks[1], (N_META, D), 1.0),
        'mix_norm_even': gain(ks[2], (PE, D)),
        'w_in_even': nrm(ks[3], (PE, D, EVEN_IN), D ** -0.5),
        'conv_w': nrm(ks[4], (PE, CONV_WIDTH, CONV_CH), CONV_WIDTH ** -0.5),
        'conv_b': nrm(ks[5], (PE, CONV_CH), 0.01),
        'conv_ln_g': gain(ks[6], (PE, CONV_CH)),
        'conv_ln_b': nrm(ks[7], (PE, CONV_CH), 0.01),
        'q_norm_g': gain(ks[8], (PE, SB_HEAD_DIM)),
        'k_norm_g': gain(ks[9], (PE, SB_HEAD_DIM)),
        'w_out_even': nrm(ks[10], (PE, EVEN_MIX, D), EVEN_MIX ** -0.5),
        'ffn_norm_even': gain(ks[11], (PE, D)),
        'ffn_w_gate': nrm(ks[12], (PE, D, D_FF), D ** -0.5),
        'ffn_w_up': nrm(ks[13], (PE, D, D_FF), D ** -0.5),
        'ffn_w_down': nrm(ks[14], (PE, D_FF, D), D_FF ** -0.5),
        'mix_norm_odd': gain(ks[15], (PO, D)),
        'w_in_odd': nrm(ks[16], (PO, D, 2 * LRU_WIDTH), D ** -0.5),
        'lru_conv_w': nrm(ks[17], (PO, LRU_CONV_WIDTH, LRU_WIDTH), LRU_CONV_WIDTH ** -0.5),
        'lru_conv_b': nrm(ks[18], (PO, LRU_WIDTH), 0.01),
        'gate_r_w': nrm(ks[19], (PO, LRU_BLOCKS, LRU_BLOCK_DIM, LRU_BLOCK_DIM), LRU_BLOCK_DIM ** -0.5),
        'gate_r_b': nrm(ks[20], (PO, LRU_WIDTH), 0.01),
        'gate_i_w': nrm(ks[21], (PO, LRU_BLOCKS, LRU_BLOCK_DIM, LRU_BLOCK_DIM), LRU_BLOCK_DIM ** -0.5),
        'gate_i_b': nrm(ks[22], (PO, LRU_WIDTH), 0.01),
        'lru_lambda': lru_lambda,
        'w_out_odd': nrm(ks[23], (PO, LRU_WIDTH, D), LRU_WIDTH ** -0.5),
        'ffn_norm_odd': gain(ks[24], (PO, D)),
        'router_w': nrm(ks[25], (PO, D, N_EXPERTS), D ** -0.5),
        'moe_w_gate': nrm(ks[27], (PO, N_EXPERTS, D, D_FF_EXPERT), D ** -0.5),
        'moe_w_up': nrm(ks[28], (PO, N_EXPERTS, D, D_FF_EXPERT), D ** -0.5),
        'moe_w_down': nrm(ks[29], (PO, N_EXPERTS, D_FF_EXPERT, D), D_FF_EXPERT ** -0.5),
    }

def reference(x, meta_tokens, mix_norm_even, w_in_even, conv_w, conv_b, conv_ln_g, conv_ln_b,
              q_norm_g, k_norm_g, w_out_even, ffn_norm_even, ffn_w_gate, ffn_w_up, ffn_w_down,
              mix_norm_odd, w_in_odd, lru_conv_w, lru_conv_b, gate_r_w, gate_r_b, gate_i_w, gate_i_b,
              lru_lambda, w_out_odd, ffn_norm_odd, router_w, moe_w_gate, moe_w_up, moe_w_down):
    b = x.shape[0]
    meta = jnp.broadcast_to(meta_tokens[None].astype(x.dtype), (b, N_META, D_MODEL))
    h = jnp.concatenate([meta, x], axis=1)
    for layer in range(DEPTH):
        p = layer // 2
        if layer % 2 == 0:
            h = h + conv_sb_mixer(h, mix_norm_even[p], w_in_even[p], conv_w[p], conv_b[p],
                                  conv_ln_g[p], conv_ln_b[p], q_norm_g[p], k_norm_g[p], w_out_even[p])
            h = h + swiglu(rms_norm(h, ffn_norm_even[p]), ffn_w_gate[p], ffn_w_up[p], ffn_w_down[p])
        else:
            h = h + rglru_mixer(h, mix_norm_odd[p], w_in_odd[p], lru_conv_w[p], lru_conv_b[p],
                                gate_r_w[p], gate_r_b[p], gate_i_w[p], gate_i_b[p], lru_lambda[p],
                                w_out_odd[p])
            h = h + moe_swiglu(rms_norm(h, ffn_norm_odd[p]), router_w[p], moe_w_gate[p],
                               moe_w_up[p], moe_w_down[p])
    return h[:, N_META:]


_drawn_inputs = setup_inputs


def setup_inputs(seed=0):
    import zlib

    import numpy as np

    out = dict(_drawn_inputs(seed))
    spreads = {}
    factors = {'conv_ln_b': 3.759, 'q_norm_g': 2.806, 'gate_r_b': 31.391, 'gate_i_b': 8.0}
    for name, (base, spread) in spreads.items():
        noise = np.random.default_rng([zlib.crc32(name.encode()), seed]).standard_normal(out[name].shape)
        drawn = base * np.exp(spread * noise) if base else spread * noise
        out[name] = __import__('jax').numpy.asarray(drawn.astype(out[name].dtype))
    for name, factor in factors.items():
        out[name] = (out[name] * factor).astype(out[name].dtype)
    return out
```

```python
import numpy as np
import concourse.bass as bass
from concourse import mybir
from contextlib import ExitStack

F32 = mybir.dt.float32
F32R = mybir.dt.float32r
I32 = mybir.dt.int32
ALU = mybir.AluOpType
ACT = mybir.ActivationFunctionType
AX = mybir.AxisListType

D = 1024
SEQ = 256
META = 16
T = SEQ + META
KD = D // 128
EPS = 1e-6
CONV_CH = 512
CONV_W = 31
HEADS = 8
HD = 64
CT = CONV_CH // 128
EVEN_IN = 2560
D_FF = 2688
KF = D_FF // 128
LRU = 1408
KL = LRU // 128
LRU_BLOCK = 88
LRU_CONV = 4
NE = 8
FE = 3584
STEPS = FE // 512
CHUNK = 128

VEC = {}
_at = 0
for _name, _n in (("mix_norm_even", KD), ("ffn_norm_even", KD), ("mix_norm_odd", KD), ("conv_w", CONV_W * CT),
                  ("conv_b", CT), ("ln_g", CT), ("ln_b", CT), ("q_g", 1), ("k_g", 1), ("lru_conv_w", LRU_CONV * KL),
                  ("lru_conv_b", KL), ("r_b", KL), ("i_b", KL), ("lam", KL), ("router", KD * NE)):
    VEC[_name] = (_at, _n)
    _at += _n
NVEC = _at

QSTART = (0, 128, 256)
KSTART = (0, 128, T - 128)
QCOUNT = tuple(T - q for q in QSTART)
QOFF = (0, QCOUNT[0], QCOUNT[0] + QCOUNT[1])
NS = sum(QCOUNT)
CON = {}
_at = 0
for _name, _n in (("ident", 128), ("ones", 128), ("headblk", 128), ("tri_ge", 128), ("tri_lt", 128), ("iota", 128),
                  ("mask", NS), ("negmask", NS), ("tie", NE * NE), ("erow", NE), ("zero8", NE)):
    CON[_name] = (_at, _n)
    _at += _n
NCON = _at


def shape_constants():
    c = np.zeros((128, NCON), np.float32)
    p = np.arange(128)[:, None]
    m = np.arange(128)[None, :]

    def put(name, a):
        c[:, CON[name][0]:CON[name][0] + CON[name][1]] = a

    put("ident", p == m)
    put("ones", 1.0)
    put("headblk", p // HD == m // HD)
    put("tri_ge", p >= m)
    put("tri_lt", p < m)
    put("iota", m)
    mask = np.zeros((128, NS), np.float32)
    for ch in range(3):
        key = KSTART[ch] + p
        query = np.arange(QSTART[ch], T)[None, :]
        mask[:, QOFF[ch]:QOFF[ch] + QCOUNT[ch]] = (key < query) & (key >= 128 * ch)
    put("mask", mask)
    put("negmask", -mask)
    e = np.arange(NE)
    put("tie", (e[None, :] < e[:, None]).reshape(1, -1))
    put("erow", e[None, :])
    return c


def band_inputs(m):
    return [i for i in (m - 1, m, m + 1) if 0 <= i < KL]


BAND_UNITS = [[m for m in (2 * j, 2 * j + 1) if m < KL] for j in range((KL + 1) // 2)]
BAND_TILES = [(m, g, i) for ms in BAND_UNITS for m in ms for g in range(2) for i in band_inputs(m)]


def unit_table():
    units = []
    for c in range(2):
        units.append(("w_in_even", 256 * c, KD, 256))
        units.append(("w_in_even", CONV_CH + 256 * c, KD, 256))
    for c in range(4):
        units.append(("w_in_even", 2 * CONV_CH + 256 * c, KD, 256))
    units.append(("w_v", 0, KD // 2, 512))
    units.append(("w_v", KD // 2, KD // 2, 512))
    for c in range(4):
        units.append(("w_out_even", 256 * c, KD, 256))
    for c in range((KF + 1) // 2):
        w = min(256, D_FF - 256 * c)
        units.append(("ffn_w_gate", 256 * c, KD, w))
        units.append(("ffn_w_up", 256 * c, KD, w))
    for c in range(4):
        for k0 in range(0, KF, 8):
            units.append(("ffn_w_down", (256 * c, k0), min(8, KF - k0), 256))
    for base in (LRU, 0):
        for c in range((KL + 1) // 2):
            units.append(("w_in_odd", base + 256 * c, KD, min(256, LRU - 256 * c)))
    at = 0
    for ms in BAND_UNITS:
        n = sum(2 * len(band_inputs(m)) for m in ms)
        units.append(("band", at, n, 128))
        at += n
    for k0 in range(0, KL, 2):
        units.append(("w_out_odd", k0, min(2, KL - k0), D))
    return units


UNITS = unit_table()
U_CONV, U_Q, U_K, U_V, U_OUT_E = 0, 4, 6, 8, 10
U_FFN1 = 14
U_FFN2 = U_FFN1 + 2 * ((KF + 1) // 2)
U_XB = U_FFN2 + 12
U_GATE = U_XB + (KL + 1) // 2
U_BAND = U_GATE + (KL + 1) // 2
U_OUT_O = U_BAND + len(BAND_UNITS)
U_MOE = U_OUT_O + (KL + 1) // 2
assert U_MOE == len(UNITS)

RAW = 7
SPLIT = 3
WIDTH = 2048
PER_ITEM = 6 * STEPS
assert PER_ITEM % RAW == 0 and PER_ITEM % SPLIT == 0
MAX_EXTRA = 3
ITEMS = NE + MAX_EXTRA + 1


def g_unit(s):
    return 0 if s == 0 else 4 + 6 * (s - 1)


def u_unit(s):
    return g_unit(s) + 2


def d_unit(s):
    return 8 + 6 * s if s < STEPS - 1 else PER_ITEM - 2


def trunk_kernel(nc, a, out):
    base = [(nc.sbuf_base + 63) // 64 * 64]
    ctx = ExitStack()

    def sb(name, shape, dt=F32):
        n = 4
        for s in shape[1:]:
            n *= s
        t = nc.alloc_sbuf_tensor_at(name, shape, dt, offset=base[0])
        base[0] += (n + 31) // 32 * 32
        return t

    with ctx:
        raw = [sb(f"raw{i}", [128, WIDTH]) for i in range(RAW)]
        whi = [sb(f"whi{i}", [128, WIDTH], F32R) for i in range(SPLIT)]
        wlo = [sb(f"wlo{i}", [128, WIDTH], F32R) for i in range(SPLIT)]
        con = sb("con", [128, NCON])
        vec = sb("vec", [128, NVEC])
        top = base[0]

        h = sb("h", [128, KD, T])
        hn_top = base[0]
        hn_hi = sb("hn_hi", [128, KD, T], F32R)
        hn_lo = sb("hn_lo", [128, KD, T], F32R)
        scr = sb("scr", [128, KD, T])
        rt = sb("rt", [128, 2, T])
        rs = sb("rs", [128, 2, T])
        phase = base[0]
        mix_hi = sb("mix_hi", [128, KD, T], F32R)
        mix_lo = sb("mix_lo", [128, KD, T], F32R)
        qf = sb("qf", [128, CT, T])
        kf = sb("kf", [128, CT, T])
        vf = sb("vf", [128, 3, 512])
        uin = sb("uin", [128, CT, T])
        cacc = sb("cacc", [128, CT, T])
        sg = sb("sg", [128, 2, T])
        zm = sb("zm", [128, 2, NS])
        lx = sb("lx", [128, 2, NS])
        ll = sb("ll", [128, 2, NS])
        ww = sb("ww", [128, 2, NS])
        e_end = base[0]
        base[0] = phase
        hid_hi = sb("hid_hi", [128, KF, T], F32R)
        hid_lo = sb("hid_lo", [128, KF, T], F32R)
        fsg = sb("fsg", [128, 2, T])
        fh = sb("fh", [128, 2, T])
        f_end = base[0]
        base[0] = phase
        xb_hi = sb("xb_hi", [128, KL, T], F32R)
        xb_lo = sb("xb_lo", [128, KL, T], F32R)
        gg = sb("gg", [128, KL, SEQ])
        rg = sb("rg", [128, KL, T])
        ig = sb("ig", [128, KL, T])
        xbf = sb("xbf", [128, 2, T])
        c8 = sb("c8", [128, KL])
        c8n = sb("c8n", [128, KL])
        sp_t = sb("sp_t", [128, 4, KL])
        o_end = base[0]
        base[0] = hn_top
        tt = sb("tt", [128, KL, T])
        base[0] = top + 4 * KD * T
        acc = sb("acc", [128, 2, D])
        gain = sb("gain", [128, D])
        xs = sb("xs", [128, 2, D])
        xnt = sb("xnt", [128, KD, SEQ])
        xe_hi = sb("xe_hi", [128, KD, CHUNK], F32R)
        xe_lo = sb("xe_lo", [128, KD, CHUNK], F32R)
        silu = sb("silu", [128, 2, 512])
        hb = sb("hb", [128, 2, 512])
        ht_hi = sb("ht_hi", [128, 2, 512], F32R)
        ht_lo = sb("ht_lo", [128, 2, 512], F32R)
        ys = sb("ys", [128, D])
        sel_m = sb("sel_m", [128, 2, CHUNK])
        sel_t = sb("sel_t", [128, 2 * CHUNK])
        sq = sb("sq", [128, D])
        st = sb("st", [128, 16])
        lg = sb("lg", [128, 2, NE])
        cmpa = sb("cmpa", [128, 2 * NE, NE])
        cmpb = sb("cmpb", [128, 2 * NE, NE])
        rank = sb("rank", [128, 2, NE])
        chosen = sb("chosen", [128, 2, NE])
        ex = sb("ex", [128, 2, NE])
        gates = sb("gates", [128, 2, NE])
        pos = sb("pos", [128, 2, NE])
        count = sb("count", [128, NE])
        over = sb("over", [128, NE])
        cum = sb("cum", [128, NE])
        pick = sb("pick", [128, MAX_EXTRA + 1, NE])
        tmp8 = sb("tmp8", [128, 2, NE])
        item_pos = sb("item_pos", [128, 2, ITEMS])
        item_gate = sb("item_gate", [128, 2, ITEMS])
        head_f = sb("head_f", [1, 8])
        head_i = sb("head_i", [1, 8], I32)
        m_end = base[0]
        assert max(e_end, f_end, o_end, m_end) <= nc.sbuf_usable_end, (top, e_end, f_end, o_end, m_end)

        P = ctx.enter_context(nc.psum_tensor("P", [128, 8, 512], F32))

        def cst(name):
            o, n = CON[name]
            return con[:, o:o + n]

        def v(name, i=0, n=1):
            o = VEC[name][0] + i
            return vec[:, o:o + n]

        def sem(name):
            return ctx.enter_context(nc.semaphore(name))

        params_in = sem("params_in")
        h_in = sem("h_in")
        gain_in = sem("gain_in")
        raw_full = [sem(f"raw_full{i}") for i in range(RAW)]
        hi_ready = sem("hi_ready")
        lo_ready = sem("lo_ready")
        unit_used = sem("unit_used")
        sq_ready, ss_ready, inv_ready, root_ready, nf_ready, nhi_ready, norm_ready = (
            sem(n) for n in ("sq_ready", "ss_ready", "inv_ready", "root_ready", "nf_ready", "nhi_ready", "norm_ready"))
        dve_step = sem("dve_step")
        act_step = sem("act_step")
        sig_ready = sem("sig_ready")
        uin_ready = sem("uin_ready")
        conv_step = sem("conv_step")
        qk_copied = sem("qk_copied")
        qk_squared = sem("qk_squared")
        v_copied = sem("v_copied")
        qk_ss, qk_inv, qk_root, qk_normed = (sem(n) for n in ("qk_ss", "qk_inv", "qk_root", "qk_normed"))
        z_done, zm_ready, ln_ready, l_ready, r_done, wz_ready, wexp_ready, w_ready, pv_done = (
            sem(n) for n in ("z_done", "zm_ready", "ln_ready", "l_ready", "r_done", "wz_ready", "wexp_ready",
                             "w_ready", "pv_done"))
        attn_hi, attn_lo = sem("attn_hi"), sem("attn_lo")
        mean_done, xc_ready, xsq_ready, var_done, var_inv, var_root, ln_scaled, ln_silu, ln_hi, ln_lo = (
            sem(n) for n in ("mean_done", "xc_ready", "xsq_ready", "var_done", "var_inv", "var_root", "ln_scaled",
                             "ln_silu", "ln_hi", "ln_lo"))
        added_e = sem("added_e")
        ffn_silu, ffn_h, ffn_hi, ffn_lo, added_f = (sem(n) for n in ("ffn_silu", "ffn_h", "ffn_hi", "ffn_lo", "added_f"))
        xb_ready, xb_hi_ready, xb_lo_ready, gelu_ready, gates_ready = (
            sem(n) for n in ("xb_ready", "xb_hi_ready", "xb_lo_ready", "gelu_ready", "gates_ready"))
        lam_exp, lam_ready = sem("lam_exp"), sem("lam_ready")
        tanh_ready, decay_ready, ratio_ready, bscale_ready, xi_sum, xi_ready = (
            sem(n) for n in ("tanh_ready", "decay_ready", "ratio_ready", "bscale_ready", "xi_sum", "xi_ready"))
        y_ready, y_hi_ready, y_lo_ready = sem("y_ready"), sem("y_hi_ready"), sem("y_lo_ready")
        resid_done, h2_ready, h2_sq, h2_inv, h2_root, xs_ready = (
            sem(n) for n in ("resid_done", "h2_ready", "h2_sq", "h2_inv", "h2_root", "xs_ready"))
        xt_done, xt_copied, logits_done, lmax_ready, lexp_ready, chosen_ready, slots_done, items_ready, head_ready = (
            sem(n) for n in ("xt_done", "xt_copied", "logits_done", "lmax_ready", "lexp_ready", "chosen_ready",
                             "slots_done", "items_ready", "head_ready"))
        sel_ready, gathered, xe_hi_ready, xe_ready = (sem(n) for n in ("sel_ready", "gathered", "xe_hi_ready", "xe_ready"))
        selt_done, selt_ready = sem("selt_done"), sem("selt_ready")
        silu_ready, h_ready, turned, ht_hi_ready, ht_ready = (
            sem(n) for n in ("silu_ready", "h_ready", "turned", "ht_hi_ready", "ht_ready"))
        ys_act, ys_dve, scattered, acc_added = (sem(n) for n in ("ys_act", "ys_dve", "scattered", "acc_added"))
        stored = sem("stored")

        def km(ap):
            return ap.rearrange("(k p) m -> p k m", p=128)

        view = {"w_in_even": km(a["w_in_even"][0]), "w_v": km(a["w_in_even"][0])[:, :, 2 * CONV_CH + 1024:EVEN_IN],
                "w_out_even": km(a["w_out_even"][0]), "ffn_w_gate": km(a["ffn_w_gate"][0]),
                "ffn_w_up": km(a["ffn_w_up"][0]), "ffn_w_down": km(a["ffn_w_down"][0]),
                "w_in_odd": km(a["w_in_odd"][0]), "w_out_odd": km(a["w_out_odd"][0])}

        def unit_source(u):
            name, at, k, w = UNITS[u]
            if name == "band":
                return a["band"][:, at * 128:(at + k) * 128].rearrange("p (k m) -> p k m", m=128)
            if name in ("w_v", "w_out_odd"):
                return view[name][:, at:at + k, :]
            if name == "ffn_w_down":
                return view[name][:, at[1]:at[1] + k, at[0]:at[0] + w]
            return view[name][:, 0:k, at:at + w]

        def unit_width(u):
            return UNITS[u][2] * UNITS[u][3]

        def pair(u):
            return 2 * (u % 3)

        def xsum(j):
            return rt[:, :, :] if j % 2 == 0 else rs[:, :, :]

        def turn_bank(s):
            return 1 if s == STEPS - 1 else 6 + s % 2

        def scatter_bank(n):
            return (6, 7, 4, 5)[n]

        block = ctx.enter_context(nc.Block())

        @block.sync
        def _(sp):
            sp.dma_start(h[:, :, :], a["h_t"].rearrange("p (k t) -> p k t", k=KD)).then_inc(h_in, 16)
            sp.dma_start(con[:, :], a["con"]).then_inc(params_in, 16)
            sp.dma_start(vec[:, :], a["vec"]).then_inc(params_in, 16)
            for u in range(U_MOE):
                if u >= RAW:
                    sp.wait_ge(lo_ready, u - RAW + 1)
                k, w = UNITS[u][2], UNITS[u][3]
                sp.dma_start(raw[u % RAW][:, 0:k * w].rearrange("p (k m) -> p k m", k=k), unit_source(u))\
                    .then_inc(raw_full[u % RAW], 16)

            w_gate = a["moe_w_gate"][0].rearrange("e (k p) f -> e p k f", p=128)
            w_up = a["moe_w_up"][0].rearrange("e (k p) f -> e p k f", p=128)
            w_down = a["moe_w_down"][0].rearrange("e (k p) m -> e p k m", p=128)

            def load_expert(i, e):
                def load(k, src, kk):
                    u = U_MOE + k
                    sp.wait_ge(lo_ready, PER_ITEM * i + (u - RAW + 1))
                    sp.dma_start(raw[u % RAW][:, :].rearrange("p (k m) -> p k m", k=kk), src)\
                        .then_inc(raw_full[u % RAW], 16)

                for s in range(STEPS + 1):
                    if s < STEPS:
                        f = slice(512 * s, 512 * s + 512)
                        for half in range(2):
                            load(g_unit(s) + half, w_gate[e, :, 4 * half:4 * half + 4, f], 4)
                        for half in range(2):
                            load(u_unit(s) + half, w_up[e, :, 4 * half:4 * half + 4, f], 4)
                    if s >= 1:
                        for half in range(2):
                            k0 = 4 * (s - 1) + 2 * half
                            load(d_unit(s - 1) + half, w_down[e, :, k0:k0 + 2, :], 2)

            with sp.Fori(0, NE) as i:
                load_expert(i, i)
            sp.wait_ge(head_ready, 1)
            extra = sp.value_load(head_i[0:1, 0:1], min_val=0, max_val=MAX_EXTRA)
            with sp.If(extra > 0):
                with sp.Fori(0, extra) as j:
                    e = sp.value_load(head_i[0:1, bass.ds(j + 1, 1)], min_val=0, max_val=NE - 1)
                    load_expert(j + NE, e)
            sp.wait_ge(acc_added, 4 * extra + 4 * NE)
            sp.dma_start(out[0].rearrange("(c p) d -> p c d", p=128), acc[:, :, :]).then_inc(stored, 16)
            sp.wait_ge(stored, 16)

        @block.gpsimd
        def _(pool):
            for hd in range(HEADS):
                pool.wait_ge(wexp_ready, hd + 1)
                if hd >= 2:
                    pool.wait_ge(pv_done, hd - 1)
                pool.tensor_tensor(ww[:, hd % 2], lx[:, hd % 2], cst("mask"), ALU.mult).then_inc(w_ready, 1)
            for j, ms in enumerate(BAND_UNITS):
                m0, n = ms[0], len(ms)
                if j >= 2:
                    pool.wait_ge(xi_ready, j - 1)
                pool.wait_ge(xb_lo_ready, j + 1)
                pool.tensor_tensor(xsum(j)[:, 0:n], xb_hi[:, m0:m0 + n].bitcast(F32), xb_lo[:, m0:m0 + n].bitcast(F32),
                                   ALU.add).then_inc(xi_sum, 1)
                pool.wait_ge(xi_sum, j + 1)
                pool.wait_ge(gates_ready, j + 1)
                pool.tensor_tensor(ig[:, m0:m0 + n], ig[:, m0:m0 + n], xsum(j)[:, 0:n], ALU.mult).then_inc(xi_ready, 1)

        @block.scalar
        def _(act):
            steps = [0]

            def step(ins):
                steps[0] += 1
                ins.then_inc(act_step, 1)
                act.wait_ge(act_step, steps[0])

            def split_hi(u):
                act.wait_ge(raw_full[u % RAW], 16 * (u // RAW + 1))
                if u >= SPLIT:
                    act.wait_ge(unit_used, u - SPLIT + 1)
                w = unit_width(u)
                act.activation(whi[u % SPLIT][:, 0:w], raw[u % RAW][:, 0:w], ACT.Copy).then_inc(hi_ready, 1)

            def norm_high(n):
                if n > 0:
                    act.wait_ge(added_e if n == 1 else added_f, 4)
                act.activation(scr[:, :, :], h[:, :, :], ACT.Square).then_inc(sq_ready, 1)
                act.wait_ge(inv_ready, 2 * n + 2)
                act.activation(rs[:, 0], rt[:, 0], ACT.Sqrt).then_inc(root_ready, 1)
                act.wait_ge(nf_ready, KD * (n + 1))
                act.activation(hn_hi[:, :, :], scr[:, :, :], ACT.Copy).then_inc(nhi_ready, 1)

            def after(u):
                if u in (1, 3):
                    act.wait_ge(unit_used, u + 1)
                    if u == 3:
                        act.wait_ge(uin_ready, 1)
                    act.activation(sg[:, :, :], P[:, pair(u):pair(u) + 2, 0:T], ACT.Sigmoid).then_inc(sig_ready, 1)
                elif U_Q <= u < U_V:
                    c = 2 * (u - U_Q)
                    src = qf if u < U_K else kf
                    act.wait_ge(qk_copied, u - U_Q + 1)
                    act.activation(scr[:, c:c + 2, :], src[:, c % CT:c % CT + 2, :], ACT.Square)\
                        .then_inc(qk_squared, 1)
                elif u == U_V + 1:
                    attention()
                elif u == U_OUT_E + 3:
                    norm_high(1)
                elif U_FFN1 <= u < U_FFN2 and (u - U_FFN1) % 2 == 1:
                    j = (u - U_FFN1) // 2
                    n = min(2, KF - 2 * j)
                    act.wait_ge(unit_used, u)
                    if j >= 1:
                        act.wait_ge(ffn_h, j)
                    act.activation(fsg[:, 0:n], P[:, pair(u - 1):pair(u - 1) + n, 0:T], ACT.Silu).then_inc(ffn_silu, 1)
                    act.wait_ge(ffn_h, j + 1)
                    act.activation(hid_hi[:, 2 * j:2 * j + n], fh[:, 0:n], ACT.Copy).then_inc(ffn_hi, 1)
                elif u == U_XB - 1:
                    norm_high(2)
                    step(act.activation(sp_t[:, 0], v("lam", 0, KL), ACT.Abs))
                    act.activation(sp_t[:, 0], sp_t[:, 0], ACT.Exp, scale=-1.0).then_inc(lam_exp, 1)
                elif U_XB <= u < U_GATE:
                    j = u - U_XB
                    n = min(2, KL - 2 * j)
                    act.wait_ge(xb_ready, (j + 1) * LRU_CONV * 2 if n == 2 else KL * LRU_CONV)
                    act.activation(xb_hi[:, 2 * j:2 * j + n], xbf[:, 0:n], ACT.Copy).then_inc(xb_hi_ready, 1)
                elif U_GATE <= u < U_BAND:
                    j = u - U_GATE
                    n = min(2, KL - 2 * j)
                    act.wait_ge(unit_used, u + 1)
                    act.activation(gg[:, 2 * j:2 * j + n], P[:, pair(u):pair(u) + n, 0:SEQ], ACT.Gelu_apprx_tanh)\
                        .then_inc(gelu_ready, 1)
                elif U_BAND <= u < U_OUT_O:
                    j = u - U_BAND
                    act.wait_ge(unit_used, u + 1)
                    for n, m in enumerate(BAND_UNITS[j]):
                        b = 4 * (j % 2) + 2 * n
                        act.activation(rg[:, m], P[:, b, 0:T], ACT.Sigmoid, bias=v("r_b", m))
                        last = act.activation(ig[:, m], P[:, b + 1, 0:T], ACT.Sigmoid, bias=v("i_b", m))
                    last.then_inc(gates_ready, 1)
                    if u == U_OUT_O - 1:
                        recurrence()

            def attention():
                for n in range(2 * CT):
                    act.wait_ge(qk_inv, 2 * n + 2)
                    if n >= 2:
                        act.wait_ge(qk_normed, n - 1)
                    act.activation(rs[:, n % 2], rt[:, n % 2], ACT.Sqrt, scale=1.0 / HD if n % 2 == 0 else 1.0)\
                        .then_inc(qk_root, 1)
                for hd in range(HEADS + 1):
                    if hd < HEADS:
                        b = hd % 2
                        act.wait_ge(zm_ready, hd + 1)
                        if hd >= 2:
                            act.wait_ge(w_ready, hd - 1)
                        step(act.activation(lx[:, b], zm[:, b], ACT.Abs))
                        step(act.activation(lx[:, b], lx[:, b], ACT.Exp, scale=-1.0))
                        act.activation(lx[:, b], lx[:, b], ACT.Ln, bias=1.0).then_inc(ln_ready, 1)
                    if hd >= 1:
                        b = (hd - 1) % 2
                        act.wait_ge(wz_ready, hd)
                        act.activation(lx[:, b], zm[:, b], ACT.Exp).then_inc(wexp_ready, 1)
                        if hd % 2 == 0:
                            j = hd // 2 - 1
                            act.wait_ge(pv_done, hd)
                            act.activation(mix_hi[:, CT + j], P[:, 4 + j % 2, 0:T], ACT.Copy).then_inc(attn_hi, 1)
                for c in range(CT):
                    act.wait_ge(xc_ready, c + 1)
                    act.activation(scr[:, c], cacc[:, c], ACT.Square).then_inc(xsq_ready, 1)
                act.wait_ge(var_inv, 2)
                act.activation(rs[:, 0], rt[:, 0], ACT.Sqrt).then_inc(var_root, 1)
                for c in range(CT):
                    act.wait_ge(ln_scaled, c + 1)
                    act.activation(uin[:, c], cacc[:, c], ACT.Silu, scale=v("ln_g", c), bias=v("ln_b", c))\
                        .then_inc(ln_silu, 1)
                act.wait_ge(ln_silu, CT)
                act.activation(mix_hi[:, 0:CT], uin[:, :, :], ACT.Copy).then_inc(ln_hi, 1)

            def recurrence():
                act.wait_ge(lam_ready, 1)
                act.wait_ge(gates_ready, len(BAND_UNITS))
                for m in range(KL):
                    act.activation(tt[:, m], rg[:, m], ACT.Tanh, scale=c8[:, m:m + 1]).then_inc(tanh_ready, 1)
                    act.wait_ge(tanh_ready, m + 1)
                    act.activation(rg[:, m], rg[:, m], ACT.Exp, scale=c8n[:, m:m + 1]).then_inc(decay_ready, 1)
                for m in range(KL):
                    act.wait_ge(ratio_ready, m + 1)
                    act.activation(tt[:, m], tt[:, m], ACT.Sqrt, scale=2.0).then_inc(bscale_ready, 1)
                for m in range(KL):
                    act.wait_ge(y_ready, m + 1)
                    act.activation(xb_hi[:, m, 0:SEQ], tt[:, m, META:T], ACT.Copy).then_inc(y_hi_ready, 1)

            act.wait_ge(h_in, 16)
            act.wait_ge(params_in, 32)
            norm_high(0)
            for u in range(U_MOE):
                split_hi(u)
                if u >= 2:
                    after(u - 2)
            act.wait_ge(resid_done, 1)
            act.dma_start(gain[:, :], a["gain"].to_broadcast([128, D])).then_inc(gain_in, 16)
            for c in range(2):
                for half in range(2):
                    act.wait_ge(h2_ready, c + 1)
                    act.activation(sq[:, 0:512], acc[:, c, 512 * half:512 * half + 512], ACT.Square,
                                   accum_out=st[:, 2 * c + half:2 * c + half + 1]).then_inc(h2_sq, 1)
                    act.wait_ge(h2_sq, 2 * c + half + 1)
            act.wait_ge(h2_inv, 3)
            act.activation(st[:, 6:8], st[:, 4:6], ACT.Sqrt).then_inc(h2_root, 1)
            act.wait_ge(lmax_ready, 1)
            for c in range(2):
                act.activation(ex[:, c], lg[:, c], ACT.Exp, bias=st[:, 8 + c:9 + c]).then_inc(lexp_ready, 1)

            def xe_high(n):
                act.wait_ge(gathered, n + 1)
                for b in range(2):
                    last = act.activation(xe_hi[:, 4 * b:4 * b + 4], P[:, 6 + b, :].rearrange("p (k t) -> p k t", k=4),
                                          ACT.Copy)
                last.then_inc(xe_hi_ready, 1)

            xe_high(0)

            def finish(i):
                act.wait_ge(unit_used, PER_ITEM * i + (U_MOE + PER_ITEM))
                act.activation(ys[:, 0:512], P[:, 4, :], ACT.Copy).then_inc(ys_act, 1)

            def item(i, first):
                for k in range(PER_ITEM):
                    u = U_MOE + k
                    act.wait_ge(raw_full[u % RAW], 16 * (PER_ITEM // RAW) * i + 16 * (u // RAW + 1))
                    act.wait_ge(unit_used, PER_ITEM * i + (u - SPLIT + 1))
                    act.activation(whi[u % SPLIT][:, :], raw[u % RAW][:, :], ACT.Copy).then_inc(hi_ready, 1)
                    if k == 1 and not first:
                        finish(i - 1)
                    done = k - 2
                    for s in range(STEPS):
                        if done == g_unit(s) + 1:
                            if s >= 1:
                                turn_high(i, s - 1)
                            act.wait_ge(unit_used, PER_ITEM * i + (U_MOE + done + 1))
                            if s >= 2:
                                act.wait_ge(h_ready, STEPS * i + (s - 1))
                            act.activation(silu[:, s % 2], P[:, s % 2, :], ACT.Silu).then_inc(silu_ready, 1)
                    if done == u_unit(0) + 1:
                        act.wait_ge(selt_done, i + 1)
                        act.activation(sel_t[:, :], P[:, 7, 0:2 * CHUNK], ACT.Copy).then_inc(selt_ready, 1)
                    if done == d_unit(STEPS - 2) + 1:
                        turn_high(i, STEPS - 1)
                        xe_high(i + 1)

            def turn_high(i, s):
                act.wait_ge(turned, STEPS * i + (s + 1))
                if s >= 2:
                    act.wait_ge(unit_used, PER_ITEM * i + (U_MOE + d_unit(s - 2) + 2))
                act.activation(ht_hi[:, s % 2], P[:, turn_bank(s), :], ACT.Copy).then_inc(ht_hi_ready, 1)

            item(0, True)
            with act.Fori(1, NE) as i:
                item(i, False)
            act.wait_ge(head_ready, 1)
            extra = act.value_load(head_i[0:1, 0:1], min_val=0, max_val=MAX_EXTRA)
            with act.If(extra > 0):
                with act.Fori(NE, extra + NE) as i:
                    item(i, False)
            finish(extra + (NE - 1))

        @block.vector
        def _(dve):
            steps = [0]

            def step(ins):
                steps[0] += 1
                ins.then_inc(dve_step, 1)
                dve.wait_ge(dve_step, steps[0])

            def split_lo(u):
                dve.wait_ge(hi_ready, u + 1)
                w = unit_width(u)
                dve.tensor_tensor(wlo[u % SPLIT][:, 0:w], raw[u % RAW][:, 0:w], whi[u % SPLIT][:, 0:w].bitcast(F32),
                                  ALU.subtract).then_inc(lo_ready, 1)

            def inverse(dst, src, n, ready, at):
                dve.tensor_scalar(dst, src, 1.0 / n, EPS, ALU.mult, ALU.add).then_inc(ready, 1)
                dve.wait_ge(ready, at + 1)
                dve.reciprocal(dst, dst).then_inc(ready, 1)

            def norm_low(n):
                g = ("mix_norm_even", "ffn_norm_even", "mix_norm_odd")[n]
                dve.wait_ge(ss_ready, n + 1)
                inverse(rt[:, 0], P[:, 7, 0:T], D, inv_ready, 2 * n)
                dve.wait_ge(root_ready, n + 1)
                for k in range(KD):
                    dve.scalar_tensor_tensor(out=scr[:, k], in0=h[:, k], scalar=v(g, k), in1=rs[:, 0],
                                             op0=ALU.mult, op1=ALU.mult).then_inc(nf_ready, 1)
                dve.wait_ge(nf_ready, KD * (n + 1))
                dve.wait_ge(nhi_ready, n + 1)
                dve.tensor_tensor(hn_lo[:, :, :], scr[:, :, :], hn_hi[:, :, :].bitcast(F32), ALU.subtract)\
                    .then_inc(norm_ready, 1)

            conv_at = [0]

            def conv(n):
                for x in range(conv_at[0], min(conv_at[0] + n, CT * CONV_W)):
                    s, c = x // CT, x % CT
                    w = v("conv_w", (CONV_W - 1 - s) * CT + c)
                    if s == 0:
                        dve.tensor_scalar(cacc[:, c], uin[:, c], w, v("conv_b", c), ALU.mult, ALU.add)\
                            .then_inc(conv_step, 1)
                    else:
                        dve.wait_ge(conv_step, x - CT + 1)
                        dve.scalar_tensor_tensor(out=cacc[:, c, s:T], in0=uin[:, c, 0:T - s], scalar=w,
                                                 in1=cacc[:, c, s:T], op0=ALU.mult, op1=ALU.add).then_inc(conv_step, 1)
                conv_at[0] = min(conv_at[0] + n, CT * CONV_W)

            def after(u):
                if u in (1, 3):
                    c = u // 2
                    dve.wait_ge(sig_ready, c + 1)
                    dve.tensor_tensor(uin[:, 2 * c:2 * c + 2], P[:, pair(u - 1):pair(u - 1) + 2, 0:T], sg[:, :, :],
                                      ALU.mult).then_inc(uin_ready, 1)
                    if u == 3:
                        dve.wait_ge(uin_ready, 2)
                elif U_Q <= u < U_V:
                    dst = qf if u < U_K else kf
                    c = 2 * ((u - U_Q) % 2)
                    dve.wait_ge(unit_used, u + 1)
                    dve.tensor_copy(dst[:, c:c + 2], P[:, pair(u):pair(u) + 2, 0:T]).then_inc(qk_copied, 1)
                    conv(12)
                elif u == U_V:
                    conv(12)
                elif u == U_V + 1:
                    dve.wait_ge(unit_used, u + 1)
                    dve.tensor_copy(vf[:, :, :], P[:, 4:7, :]).then_inc(v_copied, 1)
                    attention()
                elif U_OUT_E <= u < U_FFN1:
                    m = 2 * (u - U_OUT_E)
                    dve.wait_ge(unit_used, u + 1)
                    dve.tensor_tensor(h[:, m:m + 2], P[:, pair(u):pair(u) + 2, 0:T], h[:, m:m + 2], ALU.add)\
                        .then_inc(added_e, 1)
                    if u == U_FFN1 - 1:
                        dve.wait_ge(added_e, 4)
                        norm_low(1)
                elif U_FFN1 <= u < U_FFN2 and (u - U_FFN1) % 2 == 1:
                    j = (u - U_FFN1) // 2
                    n = min(2, KF - 2 * j)
                    dve.wait_ge(unit_used, u + 1)
                    dve.wait_ge(ffn_silu, j + 1)
                    if j >= 1:
                        dve.wait_ge(ffn_lo, j)
                    dve.tensor_tensor(fh[:, 0:n], fsg[:, 0:n], P[:, pair(u):pair(u) + n, 0:T], ALU.mult)\
                        .then_inc(ffn_h, 1)
                    dve.wait_ge(ffn_h, j + 1)
                    dve.wait_ge(ffn_hi, j + 1)
                    dve.tensor_tensor(hid_lo[:, 2 * j:2 * j + n], fh[:, 0:n],
                                      hid_hi[:, 2 * j:2 * j + n].bitcast(F32), ALU.subtract).then_inc(ffn_lo, 1)
                elif U_FFN2 <= u < U_XB and (u - U_FFN2) % 3 == 2:
                    c = (u - U_FFN2) // 3
                    b = 2 * (c % 3)
                    dve.wait_ge(unit_used, u + 1)
                    dve.tensor_tensor(h[:, 2 * c:2 * c + 2], P[:, b:b + 2, 0:T], h[:, 2 * c:2 * c + 2], ALU.add)\
                        .then_inc(added_f, 1)
                    if c == 3:
                        dve.wait_ge(added_f, 4)
                        norm_low(2)
                        decay_rates()
                elif U_XB <= u < U_GATE:
                    lru_conv(u)
                elif u == U_OUT_O - 1:
                    recurrence()

            def attention():
                for n in range(2 * CT):
                    x, g = (qf, "q_g") if n % 2 == 0 else (kf, "k_g")
                    j = n // 2
                    dve.wait_ge(qk_ss, n + 1)
                    if n >= 2:
                        dve.wait_ge(qk_root, n - 1)
                    inverse(rt[:, n % 2], P[:, 6 + n % 2, 0:T], HD, qk_inv, 2 * n)
                    if n == 0:
                        dve.wait_ge(qk_copied, 4)
                    dve.wait_ge(qk_root, n + 1)
                    dve.scalar_tensor_tensor(out=x[:, j], in0=x[:, j], scalar=v(g), in1=rs[:, n % 2],
                                             op0=ALU.mult, op1=ALU.mult).then_inc(qk_normed, 1)
                for hd in range(HEADS + 1):
                    if hd < HEADS:
                        b = hd % 2
                        dve.wait_ge(z_done, hd + 1)
                        if hd >= 2:
                            dve.wait_ge(wexp_ready, hd - 1)
                        dve.tensor_tensor(zm[:, b], P[:, b, 0:NS], cst("mask"), ALU.mult).then_inc(zm_ready, 1)
                        conv(8)
                    if hd >= 1:
                        o = (hd - 1) % 2
                        dve.wait_ge(r_done, hd)
                        dve.tensor_tensor(zm[:, o], P[:, 2 + o, 0:NS], zm[:, o], ALU.add).then_inc(wz_ready, 1)
                    if hd < HEADS:
                        dve.wait_ge(ln_ready, hd + 1)
                        dve.wait_ge(zm_ready, hd + 1)
                        if hd >= 2:
                            dve.wait_ge(r_done, hd - 1)
                        step(dve.scalar_tensor_tensor(out=ll[:, b], in0=zm[:, b], scalar=0.0, in1=lx[:, b],
                                                      op0=ALU.max, op1=ALU.add))
                        dve.tensor_tensor(ll[:, b], ll[:, b], cst("negmask"), ALU.mult).then_inc(l_ready, 1)
                    if hd >= 2 and hd % 2 == 0:
                        attn_low(hd // 2 - 1)
                conv(CT * CONV_W)
                dve.wait_ge(mean_done, 1)
                dve.wait_ge(conv_step, CT * CONV_W)
                for c in range(CT):
                    dve.scalar_tensor_tensor(out=cacc[:, c], in0=P[:, 6, 0:T], scalar=-1.0 / CONV_CH, in1=cacc[:, c],
                                             op0=ALU.mult, op1=ALU.add).then_inc(xc_ready, 1)
                dve.wait_ge(var_done, 1)
                inverse(rt[:, 0], P[:, 7, 0:T], CONV_CH, var_inv, 0)
                dve.wait_ge(var_root, 1)
                dve.wait_ge(xc_ready, CT)
                for c in range(CT):
                    dve.tensor_tensor(cacc[:, c], cacc[:, c], rs[:, 0], ALU.mult).then_inc(ln_scaled, 1)
                dve.wait_ge(ln_hi, 1)
                dve.tensor_tensor(mix_lo[:, 0:CT], uin[:, :, :], mix_hi[:, 0:CT].bitcast(F32), ALU.subtract)\
                    .then_inc(ln_lo, 1)

            def attn_low(j):
                dve.wait_ge(attn_hi, j + 1)
                dve.tensor_tensor(mix_lo[:, CT + j], P[:, 4 + j % 2, 0:T], mix_hi[:, CT + j].bitcast(F32),
                                  ALU.subtract).then_inc(attn_lo, 1)

            def decay_rates():
                x, s, s2, q = (sp_t[:, n] for n in range(4))
                dve.wait_ge(lam_exp, 1)
                step(dve.tensor_scalar(s, x, 2.0, None, ALU.add))
                step(dve.reciprocal(s, s))
                step(dve.tensor_tensor(s, s, x, ALU.mult))
                step(dve.tensor_tensor(s2, s, s, ALU.mult))
                terms = range(19, 1, -2)
                step(dve.tensor_scalar(q, s2, 1.0 / 21, 1.0 / 19, ALU.mult, ALU.add))
                for n in terms:
                    if n == 19:
                        continue
                    step(dve.tensor_tensor(q, q, s2, ALU.mult))
                    step(dve.tensor_scalar(q, q, 1.0 / n, None, ALU.add))
                step(dve.tensor_tensor(q, q, s2, ALU.mult))
                step(dve.tensor_scalar(q, q, 1.0, 16.0, ALU.add, ALU.mult))
                step(dve.tensor_tensor(q, q, s, ALU.mult))
                step(dve.tensor_scalar(s2, v("lam", 0, KL), -8.0, 0.0, ALU.mult, ALU.max))
                step(dve.tensor_tensor(c8[:, :], q, s2, ALU.add))
                dve.tensor_scalar(c8n[:, :], c8[:, :], -1.0, None, ALU.mult).then_inc(lam_ready, 1)

            def lru_conv(u):
                j = u - U_XB
                n = min(2, KL - 2 * j)
                dve.wait_ge(unit_used, u + 1)
                if j >= 1:
                    dve.wait_ge(xb_lo_ready, j)
                for s in range(LRU_CONV):
                    for t in range(n):
                        m = 2 * j + t
                        w = v("lru_conv_w", (LRU_CONV - 1 - s) * KL + m)
                        x = P[:, pair(u) + t, 0:T - s]
                        if s == 0:
                            ins = dve.tensor_scalar(xbf[:, t], x, w, v("lru_conv_b", m), ALU.mult, ALU.add)
                        else:
                            dve.wait_ge(xb_ready, 2 * LRU_CONV * j + n * (s - 1) + t + 1)
                            ins = dve.scalar_tensor_tensor(out=xbf[:, t, s:T], in0=x, scalar=w, in1=xbf[:, t, s:T],
                                                           op0=ALU.mult, op1=ALU.add)
                        ins.then_inc(xb_ready, 1)
                dve.wait_ge(xb_ready, 2 * LRU_CONV * j + LRU_CONV * n)
                dve.wait_ge(xb_hi_ready, j + 1)
                dve.tensor_tensor(xb_lo[:, 2 * j:2 * j + n], xbf[:, 0:n], xb_hi[:, 2 * j:2 * j + n].bitcast(F32),
                                  ALU.subtract).then_inc(xb_lo_ready, 1)

            def recurrence():
                for m in range(KL):
                    d = rt[:, 0] if m % 2 == 0 else rt[:, 1]
                    if m == 0:
                        dve.wait_ge(xi_ready, len(BAND_UNITS))
                    dve.wait_ge(tanh_ready, m + 1)
                    step(dve.tensor_scalar(d, tt[:, m], 1.0, None, ALU.add))
                    step(dve.reciprocal(d, d))
                    dve.tensor_tensor(tt[:, m], tt[:, m], d, ALU.mult).then_inc(ratio_ready, 1)
                for m in range(KL):
                    dve.wait_ge(bscale_ready, m + 1)
                    step(dve.tensor_tensor(ig[:, m], ig[:, m], tt[:, m], ALU.mult))
                    dve.wait_ge(decay_ready, m + 1)
                    step(dve.tensor_tensor_scan(tt[:, m], rg[:, m], ig[:, m], 0.0, ALU.mult, ALU.add))
                    if m == 0:
                        dve.wait_ge(gelu_ready, (KL + 1) // 2)
                    dve.tensor_tensor(tt[:, m, META:T], tt[:, m, META:T], gg[:, m], ALU.mult).then_inc(y_ready, 1)
                    if m >= 1:
                        y_low(m - 1)
                y_low(KL - 1)

            def y_low(m):
                dve.wait_ge(y_hi_ready, m + 1)
                dve.tensor_tensor(xb_lo[:, m, 0:SEQ], tt[:, m, META:T], xb_hi[:, m, 0:SEQ].bitcast(F32),
                                  ALU.subtract).then_inc(y_lo_ready, 1)

            dve.wait_ge(h_in, 16)
            dve.wait_ge(params_in, 32)
            norm_low(0)
            for u in range(U_MOE):
                split_lo(u)
                if u >= 2:
                    after(u - 2)

            dve.wait_ge(resid_done, 1)
            for c in range(2):
                dve.tensor_copy(acc[:, c].rearrange("p (b n) -> p b n", b=2), P[:, 2 * c:2 * c + 2, :])\
                    .then_inc(h2_ready, 1)
            dve.wait_ge(h2_sq, 4)
            dve.tensor_tensor(st[:, 4:6], st[:, 0:4:2], st[:, 1:4:2], ALU.add).then_inc(h2_inv, 1)
            dve.wait_ge(h2_inv, 1)
            inverse(st[:, 4:6], st[:, 4:6], D, h2_inv, 1)
            dve.wait_ge(h2_root, 1)
            dve.wait_ge(h2_ready, 2)
            dve.wait_ge(gain_in, 16)
            for c in range(2):
                dve.scalar_tensor_tensor(out=xs[:, c], in0=acc[:, c], scalar=st[:, 6 + c:7 + c], in1=gain[:, :],
                                         op0=ALU.mult, op1=ALU.mult).then_inc(xs_ready, 1)
            for b in range(4):
                dve.wait_ge(xt_done, b + 1)
                dve.tensor_copy(xnt[:, 2 * b:2 * b + 2], P[:, 4 + b, :].rearrange("p (k t) -> p k t", k=2))\
                    .then_inc(xt_copied, 1)
            dve.wait_ge(logits_done, 1)
            step(dve.tensor_copy(lg[:, :, :], P[:, 0, 0:2 * NE].rearrange("p (c e) -> p c e", c=2)))
            step(dve.tensor_reduce(st[:, 10:12], lg[:, :, :], AX.X, ALU.max))
            dve.tensor_scalar(st[:, 8:10], st[:, 10:12], -1.0, None, ALU.mult).then_inc(lmax_ready, 1)
            flat = lg[:, :, :].rearrange("p c e -> p (c e)")
            mine = flat.unsqueeze(2).to_broadcast([128, 2 * NE, NE])
            for c in range(2):
                other = lg[:, c].unsqueeze(1).to_broadcast([128, NE, NE])
                own = mine[:, NE * c:NE * c + NE]
                dve.tensor_tensor(cmpa[:, NE * c:NE * c + NE], other, own, ALU.is_gt)
                last = dve.tensor_tensor(cmpb[:, NE * c:NE * c + NE], other, own, ALU.is_equal)
            step(last)
            tie = cst("tie").rearrange("p (e j) -> p e j", e=NE)
            for c in range(2):
                last = dve.tensor_tensor(cmpb[:, NE * c:NE * c + NE], cmpb[:, NE * c:NE * c + NE], tie, ALU.mult)
            step(last)
            step(dve.tensor_tensor(cmpa[:, :, :], cmpa[:, :, :], cmpb[:, :, :], ALU.add))
            step(dve.tensor_reduce(rank[:, :, :].rearrange("p c e -> p (c e)"), cmpa[:, :, :], AX.X, ALU.add))
            dve.tensor_scalar(chosen[:, :, :], rank[:, :, :], 1.5, None, ALU.is_lt).then_inc(chosen_ready, 1)
            dve.wait_ge(chosen_ready, 1)
            dve.wait_ge(lexp_ready, 2)
            step(dve.tensor_tensor(ex[:, :, :], ex[:, :, :], chosen[:, :, :], ALU.mult))
            step(dve.tensor_reduce(st[:, 12:14], ex[:, :, :], AX.X, ALU.add))
            step(dve.reciprocal(st[:, 14:16], st[:, 12:14]))
            for c in range(2):
                last = dve.tensor_scalar(gates[:, c], ex[:, c], st[:, 14 + c:15 + c], None, ALU.mult)
            step(last)
            dve.wait_ge(slots_done, 1)
            step(dve.scalar_tensor_tensor(out=pos[:, :, :], in0=P[:, 1, 0:2 * NE].rearrange("p (c e) -> p c e", c=2),
                                          scalar=1.0, in1=chosen[:, :, :], op0=ALU.add, op1=ALU.mult))
            step(dve.tensor_scalar(pos[:, :, :], pos[:, :, :], -1.0, None, ALU.add))
            step(dve.tensor_copy(count[:, :], P[:, 1, 2 * NE:3 * NE]))
            step(dve.tensor_scalar(over[:, :], count[:, :], CHUNK + 0.5, None, ALU.is_gt))
            step(dve.tensor_tensor_scan(cum[:, :], over[:, :], cst("zero8"), 0.0, ALU.add, ALU.add))
            for j in range(MAX_EXTRA + 1):
                last = dve.scalar_tensor_tensor(out=pick[:, j], in0=cum[:, :], scalar=float(j + 1), in1=over[:, :],
                                                op0=ALU.is_equal, op1=ALU.mult)
            step(last)
            step(dve.tensor_copy(head_f[0:1, 0:1], cum[0:1, NE - 1:NE]))
            dve.tensor_copy(item_pos[:, :, 0:NE], pos[:, :, :])
            step(dve.tensor_copy(item_gate[:, :, 0:NE], gates[:, :, :]))
            step(dve.tensor_scalar(pos[:, :, :], pos[:, :, :], -float(CHUNK), None, ALU.add))
            for j in range(MAX_EXTRA + 1):
                for src, dst in ((pos, item_pos), (gates, item_gate)):
                    for c in range(2):
                        last = dve.tensor_tensor(tmp8[:, c], src[:, c], pick[:, j], ALU.mult)
                    step(last)
                    step(dve.tensor_reduce(dst[:, :, NE + j:NE + j + 1], tmp8[:, :, :], AX.X, ALU.add))
                step(dve.tensor_tensor(tmp8[:, 0], pick[:, j], cst("erow"), ALU.mult))
                step(dve.tensor_reduce(head_f[0:1, 1 + j:2 + j], tmp8[0:1, 0], AX.X, ALU.add))
            dve.tensor_copy(head_i[0:1, 0:5], head_f[0:1, 0:5]).then_inc(head_ready, 1)

            def make_sel(i):
                for c in range(2):
                    last = dve.tensor_scalar(sel_m[:, c], cst("iota"), item_pos[:, c, bass.ds(i, 1)], None,
                                             ALU.is_equal)
                last.then_inc(sel_ready, 1)

            def xe_low(n):
                dve.wait_ge(xe_hi_ready, n + 1)
                for b in range(2):
                    last = dve.tensor_tensor(xe_lo[:, 4 * b:4 * b + 4],
                                             P[:, 6 + b, :].rearrange("p (k t) -> p k t", k=4),
                                             xe_hi[:, 4 * b:4 * b + 4].bitcast(F32), ALU.subtract)
                last.then_inc(xe_ready, 1)

            make_sel(0)
            xe_low(0)

            def finish_rows(i):
                dve.wait_ge(unit_used, PER_ITEM * i + (U_MOE + PER_ITEM))
                dve.tensor_copy(ys[:, 512:D], P[:, 5, :]).then_inc(ys_dve, 1)

            def finish_add(i):
                for n in range(4):
                    c, half = n // 2, n % 2
                    part = acc[:, c, 512 * half:512 * half + 512]
                    dve.wait_ge(scattered, 4 * i + (n + 1))
                    dve.scalar_tensor_tensor(out=part, in0=P[:, scatter_bank(n), :],
                                             scalar=item_gate[:, c, bass.ds(i, 1)], in1=part,
                                             op0=ALU.mult, op1=ALU.add).then_inc(acc_added, 1)

            def turn_low(i, s):
                dve.wait_ge(ht_hi_ready, STEPS * i + (s + 1))
                dve.tensor_tensor(ht_lo[:, s % 2], P[:, turn_bank(s), :], ht_hi[:, s % 2].bitcast(F32), ALU.subtract)\
                    .then_inc(ht_ready, 1)

            def item(i, first):
                for k in range(PER_ITEM):
                    u = U_MOE + k
                    dve.wait_ge(hi_ready, PER_ITEM * i + (u + 1))
                    dve.tensor_tensor(wlo[u % SPLIT][:, :], raw[u % RAW][:, :], whi[u % SPLIT][:, :].bitcast(F32),
                                      ALU.subtract).then_inc(lo_ready, 1)
                    if k == 1 and not first:
                        finish_rows(i - 1)
                    done = k - 2
                    if done == g_unit(0) + 1 and not first:
                        dve.wait_ge(acc_added, 4 * i - 4)
                        finish_add(i - 1)
                    for s in range(STEPS):
                        if s >= 1 and done == g_unit(s) + 1:
                            turn_low(i, s - 1)
                        if done == u_unit(s) + 1:
                            dve.wait_ge(unit_used, PER_ITEM * i + (U_MOE + done + 1))
                            dve.wait_ge(silu_ready, STEPS * i + (s + 1))
                            if s >= 2:
                                dve.wait_ge(turned, STEPS * i + (s - 1))
                            dve.tensor_tensor(hb[:, s % 2], silu[:, s % 2], P[:, 2 + s % 2, :], ALU.mult)\
                                .then_inc(h_ready, 1)
                    if done == d_unit(0) + 1:
                        dve.wait_ge(selt_done, i + 1)
                        make_sel(i + 1)
                    if done == d_unit(STEPS - 2) + 1:
                        turn_low(i, STEPS - 1)
                        xe_low(i + 1)

            item(0, True)
            with dve.Fori(1, NE) as i:
                item(i, False)
            dve.wait_ge(head_ready, 1)
            extra = dve.value_load(head_i[0:1, 0:1], min_val=0, max_val=MAX_EXTRA)
            with dve.If(extra > 0):
                with dve.Fori(NE, extra + NE) as i:
                    item(i, False)
            finish_rows(extra + (NE - 1))
            dve.wait_ge(acc_added, 4 * extra + 4 * (NE - 1))
            finish_add(extra + (NE - 1))

        @block.tensor
        def _(pe):
            def three(dst, w_hi, w_lo, x_hi, x_lo, start, stop, weights_move=False):
                for n, (w, x) in enumerate(((w_hi, x_hi), (w_hi, x_lo), (w_lo, x_hi))):
                    lhs, rhs = (x, w) if weights_move else (w, x)
                    last = pe.matmul(dst, lhs, rhs, start=start and n == 0, stop=stop and n == 2)
                return last

            def features(u, x_hi, x_lo, bank, k0=0, start=True, stop=True, cols=slice(0, T)):
                k, w = UNITS[u][2], UNITS[u][3]
                pe.wait_ge(lo_ready, u + 1)
                n = cols.stop - cols.start
                for m in range(w // 128):
                    for kk in range(k):
                        at = kk * w + m * 128
                        last = three(P[:, bank + m, 0:n], whi[u % SPLIT][:, at:at + 128], wlo[u % SPLIT][:, at:at + 128],
                                     x_hi[:, k0 + kk, cols], x_lo[:, k0 + kk, cols], start and kk == 0,
                                     stop and kk == k - 1)
                last.then_inc(unit_used, 1)

            def norm_sums(n):
                pe.wait_ge(sq_ready, n + 1)
                for k in range(KD):
                    last = pe.matmul(P[:, 7, 0:T], cst("ones"), scr[:, k], start=k == 0, stop=k == KD - 1)
                last.then_inc(ss_ready, 1)
                pe.wait_ge(norm_ready, n + 1)

            pe.wait_ge(params_in, 32)
            norm_sums(0)
            for u in range(U_V):
                if u == 3:
                    pe.wait_ge(uin_ready, 1)
                if u == 5 or u == 6:
                    pe.wait_ge(uin_ready, 2)
                if u == 4:
                    pe.wait_ge(uin_ready, 1)
                if u == 7:
                    pe.wait_ge(qk_copied, 1)
                    pe.wait_ge(qk_squared, 1)
                features(u, hn_hi, hn_lo, pair(u))
            pe.wait_ge(qk_copied, 2)
            pe.wait_ge(qk_squared, 2)
            for u in (U_V, U_V + 1):
                pe.wait_ge(lo_ready, u + 1)
                for kk in range(4):
                    k = 4 * (u - U_V) + kk
                    for c in range(3):
                        tok = slice(KSTART[c], KSTART[c] + 128)
                        last = three(P[:, 4 + c, :], whi[u % SPLIT][:, 512 * kk:512 * kk + 512],
                                     wlo[u % SPLIT][:, 512 * kk:512 * kk + 512], hn_hi[:, k, tok], hn_lo[:, k, tok],
                                     k == 0, k == KD - 1, weights_move=True)
                last.then_inc(unit_used, 1)
            pe.wait_ge(qk_squared, 4)
            pe.wait_ge(v_copied, 1)
            for n in range(2 * CT):
                if n >= 2:
                    pe.wait_ge(qk_inv, 2 * n - 3)
                pe.matmul(P[:, 6 + n % 2, 0:T], cst("headblk"), scr[:, CT * (n % 2) + n // 2], start=True, stop=True)\
                    .then_inc(qk_ss, 1)
            pe.wait_ge(qk_copied, 4)

            def scores(hd):
                j, r = hd // 2, slice(HD * (hd % 2), HD * (hd % 2) + HD)
                pe.wait_ge(qk_normed, 2 * j + 2)
                if hd >= 2:
                    pe.wait_ge(zm_ready, hd - 1)
                for c in range(3):
                    last = pe.matmul(P[:, hd % 2, QOFF[c]:QOFF[c] + QCOUNT[c]], kf[r, j, KSTART[c]:KSTART[c] + 128],
                                     qf[r, j, QSTART[c]:T], start=True, stop=True)
                last.then_inc(z_done, 1)

            def later(hd):
                b = hd % 2
                pe.wait_ge(l_ready, hd + 1)
                if hd >= 2:
                    pe.wait_ge(wz_ready, hd - 1)
                for c in range(3):
                    for o in range(c, 3):
                        skip = QSTART[o] - QSTART[c]
                        last = pe.matmul(P[:, 2 + b, QOFF[c] + skip:QOFF[c] + QCOUNT[c]],
                                         cst("tri_ge") if o == c else cst("ones"),
                                         ll[:, b, QOFF[o]:QOFF[o] + QCOUNT[o]], start=o == c, stop=o == 2)
                last.then_inc(r_done, 1)

            def values(hd):
                r = slice(HD * (hd % 2), HD * (hd % 2) + HD)
                j = hd // 2
                pe.wait_ge(w_ready, hd + 1)
                if hd >= 4 and hd % 2 == 0:
                    pe.wait_ge(attn_lo, j - 1)
                for c in range(3):
                    last = pe.matmul(P[r, 4 + j % 2, QSTART[c]:T], vf[:, c, HD * hd:HD * hd + HD],
                                     ww[:, hd % 2, QOFF[c]:QOFF[c] + QCOUNT[c]], start=c == 0, stop=c == 2)
                last.then_inc(pv_done, 1)

            scores(0)
            for hd in range(HEADS + 1):
                if hd + 1 < HEADS:
                    scores(hd + 1)
                if hd < HEADS:
                    later(hd)
                if hd >= 1:
                    values(hd - 1)
            pe.wait_ge(conv_step, CT * CONV_W)
            for c in range(CT):
                last = pe.matmul(P[:, 6, 0:T], cst("ones"), cacc[:, c], start=c == 0, stop=c == CT - 1)
            last.then_inc(mean_done, 1)
            pe.wait_ge(xsq_ready, CT)
            for c in range(CT):
                last = pe.matmul(P[:, 7, 0:T], cst("ones"), scr[:, c], start=c == 0, stop=c == CT - 1)
            last.then_inc(var_done, 1)
            pe.wait_ge(ln_lo, 1)
            pe.wait_ge(attn_lo, CT)
            for u in range(U_OUT_E, U_FFN1):
                if u == U_OUT_E + 3:
                    pe.wait_ge(added_e, 1)
                features(u, mix_hi, mix_lo, pair(u))
            norm_sums(1)
            for u in range(U_FFN1, U_FFN2):
                j = (u - U_FFN1) // 2
                if u - 3 >= U_FFN1:
                    pe.wait_ge(ffn_h, (u - 3 - U_FFN1) // 2 + 1)
                features(u, hn_hi, hn_lo, pair(u))
            for u in range(U_FFN2, U_XB):
                c, part = (u - U_FFN2) // 3, (u - U_FFN2) % 3
                if u == U_FFN2:
                    pe.wait_ge(ffn_lo, (KF + 1) // 2)
                if c == 3 and part == 0:
                    pe.wait_ge(added_f, 1)
                features(u, hid_hi, hid_lo, 2 * (c % 3), k0=8 * part, start=part == 0, stop=part == 2)
            norm_sums(2)
            for u in range(U_XB, U_GATE):
                if u - 3 >= U_XB:
                    pe.wait_ge(xb_lo_ready, u - 3 - U_XB + 1)
                features(u, hn_hi, hn_lo, pair(u))
            for u in range(U_GATE, U_BAND):
                if u - 3 >= U_GATE:
                    pe.wait_ge(gelu_ready, u - 3 - U_GATE + 1)
                else:
                    pe.wait_ge(xb_lo_ready, u - 3 - U_XB + 1)
                features(u, hn_hi, hn_lo, pair(u), cols=slice(META, T))
            pe.wait_ge(gelu_ready, (KL + 1) // 2)
            pe.wait_ge(xb_lo_ready, (KL + 1) // 2)
            for u in range(U_BAND, U_OUT_O):
                j = u - U_BAND
                pe.wait_ge(lo_ready, u + 1)
                if j >= 2:
                    pe.wait_ge(gates_ready, j - 1)
                at = 0
                for n, m in enumerate(BAND_UNITS[j]):
                    for g in range(2):
                        near = band_inputs(m)
                        for x in near:
                            last = three(P[:, 4 * (j % 2) + 2 * n + g, 0:T], whi[u % SPLIT][:, at:at + 128],
                                         wlo[u % SPLIT][:, at:at + 128], xb_hi[:, x], xb_lo[:, x],
                                         x == near[0], x == near[-1])
                            at += 128
                last.then_inc(unit_used, 1)
            pe.wait_ge(gates_ready, len(BAND_UNITS))
            for u in range(U_OUT_O, U_MOE):
                pe.wait_ge(lo_ready, u + 1)
                for kk in range(UNITS[u][2]):
                    m = 2 * (u - U_OUT_O) + kk
                    pe.wait_ge(y_lo_ready, m + 1)
                    for c in range(2):
                        for half in range(2):
                            at = D * kk + 512 * half
                            last = three(P[:, 2 * c + half, :], whi[u % SPLIT][:, at:at + 512],
                                         wlo[u % SPLIT][:, at:at + 512], xb_hi[:, m, 128 * c:128 * c + 128],
                                         xb_lo[:, m, 128 * c:128 * c + 128], m == 0, False, weights_move=True)
                last.then_inc(unit_used, 1)
            for c in range(2):
                for k in range(KD):
                    last = pe.matmul(P[:, 2 * c + k // 4, 128 * (k % 4):128 * (k % 4) + 128],
                                     h[:, k, META + 128 * c:META + 128 * c + 128], cst("ident"), start=False,
                                     stop=k % 4 == 3)
            last.then_inc(resid_done, 1)
            pe.wait_ge(xs_ready, 2)
            for b in range(4):
                for kk in range(2):
                    for c in range(2):
                        k = 2 * b + kk
                        last = pe.matmul(P[:, 4 + b, 256 * kk + 128 * c:256 * kk + 128 * c + 128],
                                         xs[:, c, 128 * k:128 * k + 128], cst("ident"), start=True, stop=True)
                last.then_inc(xt_done, 1)
            pe.wait_ge(xt_copied, 4)
            for c in range(2):
                for k in range(KD):
                    last = pe.matmul(P[:, 0, NE * c:NE * c + NE], xnt[:, k, 128 * c:128 * c + 128],
                                     v("router", NE * k, NE), start=k == 0, stop=k == KD - 1)
            last.then_inc(logits_done, 1)
            pe.wait_ge(chosen_ready, 1)
            pe.matmul(P[:, 1, 0:NE], cst("tri_lt"), chosen[:, 0], start=True, stop=True)
            pe.matmul(P[:, 1, NE:2 * NE], cst("ones"), chosen[:, 0], start=True, stop=False)
            pe.matmul(P[:, 1, NE:2 * NE], cst("tri_lt"), chosen[:, 1], start=False, stop=True)
            pe.matmul(P[:, 1, 2 * NE:3 * NE], cst("ones"), chosen[:, 0], start=True, stop=False)
            pe.matmul(P[:, 1, 2 * NE:3 * NE], cst("ones"), chosen[:, 1], start=False, stop=True)\
                .then_inc(slots_done, 1)

            def gather(i):
                pe.wait_ge(sel_ready, i + 1)
                for k in range(KD):
                    for c in range(2):
                        last = pe.matmul(P[:, 6 + k // 4, 128 * (k % 4):128 * (k % 4) + 128],
                                         xs[:, c, 128 * k:128 * k + 128], sel_m[:, c], start=c == 0, stop=c == 1)
                last.then_inc(gathered, 1)

            def in_features(i, k_unit, bank):
                for half in range(2):
                    u = U_MOE + k_unit + half
                    pe.wait_ge(lo_ready, PER_ITEM * i + (u + 1))
                    for kk in range(4):
                        k = 4 * half + kk
                        w = slice(512 * kk, 512 * kk + 512)
                        last = three(P[:, bank, :], whi[u % SPLIT][:, w], wlo[u % SPLIT][:, w], xe_hi[:, k], xe_lo[:, k],
                                     k == 0, k == KD - 1, weights_move=True)
                    last.then_inc(unit_used, 1)

            def turn(i, s):
                pe.wait_ge(h_ready, STEPS * i + (s + 1))
                if s >= 2:
                    pe.wait_ge(ht_ready, STEPS * i + (s - 1))
                for n in range(4):
                    last = pe.matmul(P[:, turn_bank(s), 128 * n:128 * n + 128], hb[:, s % 2, 128 * n:128 * n + 128],
                                     cst("ident"), is_transpose=True, start=True, stop=True)
                last.then_inc(turned, 1)

            def down(i, s):
                pe.wait_ge(ht_ready, STEPS * i + (s + 1))
                for half in range(2):
                    u = U_MOE + d_unit(s) + half
                    pe.wait_ge(lo_ready, PER_ITEM * i + (u + 1))
                    for kk in range(2):
                        n = 2 * half + kk
                        for o in range(2):
                            at = D * kk + 512 * o
                            last = three(P[:, 4 + o, :], whi[u % SPLIT][:, at:at + 512], wlo[u % SPLIT][:, at:at + 512],
                                         ht_hi[:, s % 2, 128 * n:128 * n + 128], ht_lo[:, s % 2, 128 * n:128 * n + 128],
                                         s == 0 and n == 0, s == STEPS - 1 and n == 3, weights_move=True)
                    last.then_inc(unit_used, 1)

            def scatter(i):
                pe.wait_ge(ys_act, i + 1)
                pe.wait_ge(ys_dve, i + 1)
                for n in range(4):
                    c, half = n // 2, n % 2
                    pe.matmul(P[:, scatter_bank(n), :], sel_t[:, 128 * c:128 * c + 128],
                              ys[:, 512 * half:512 * half + 512], start=True, stop=True).then_inc(scattered, 1)

            def item(i, first):
                pe.wait_ge(xe_ready, i + 1)
                for s in range(STEPS):
                    if s >= 2:
                        pe.wait_ge(h_ready, STEPS * i + (s - 1))
                    in_features(i, g_unit(s), s % 2)
                    if s == 0 and not first:
                        scatter(i - 1)
                    if s >= 1:
                        turn(i, s - 1)
                    in_features(i, u_unit(s), 2 + s % 2)
                    if s == 0:
                        if not first:
                            pe.wait_ge(acc_added, 4 * i)
                        for c in range(2):
                            last = pe.matmul(P[:, 7, 128 * c:128 * c + 128], sel_m[:, c], cst("ident"),
                                             is_transpose=True, start=True, stop=True)
                        last.then_inc(selt_done, 1)
                    if s >= 1:
                        if s == 1:
                            pe.wait_ge(selt_ready, i + 1)
                        down(i, s - 1)
                turn(i, STEPS - 1)
                pe.wait_ge(ht_ready, STEPS * i + (STEPS - 1))
                gather(i + 1)
                down(i, STEPS - 1)

            gather(0)
            item(0, True)
            with pe.Fori(1, NE) as i:
                item(i, False)
            pe.wait_ge(head_ready, 1)
            extra = pe.value_load(head_i[0:1, 0:1], min_val=0, max_val=MAX_EXTRA)
            with pe.If(extra > 0):
                with pe.Fori(NE, extra + NE) as i:
                    item(i, False)
            scatter(extra + (NE - 1))


def _tiles(x):
    return x.reshape(-1, 128).T


def kernel(**inputs):
    import concourse.bacc as _bacc
    from concourse.bass_utils import run_bass_kernel_spmd as _run

    x = {k: np.asarray(a) for k, a in inputs.items()}
    tokens = np.concatenate([x["meta_tokens"], x["x"][0]], axis=0)
    vecs = np.zeros((128, NVEC), np.float32)

    def put(name, value):
        at, n = VEC[name]
        vecs[:, at:at + n] = value

    put("mix_norm_even", _tiles(x["mix_norm_even"][0]))
    put("ffn_norm_even", _tiles(x["ffn_norm_even"][0]))
    put("mix_norm_odd", _tiles(x["mix_norm_odd"][0]))
    put("conv_w", x["conv_w"][0].reshape(CONV_W, CT, 128).transpose(2, 0, 1).reshape(128, -1))
    put("conv_b", _tiles(x["conv_b"][0]))
    put("ln_g", _tiles(x["conv_ln_g"][0]))
    put("ln_b", _tiles(x["conv_ln_b"][0]))
    put("q_g", np.concatenate([x["q_norm_g"][0]] * 2)[:, None])
    put("k_g", np.concatenate([x["k_norm_g"][0]] * 2)[:, None])
    put("lru_conv_w", x["lru_conv_w"][0].reshape(LRU_CONV, KL, 128).transpose(2, 0, 1).reshape(128, -1))
    put("lru_conv_b", _tiles(x["lru_conv_b"][0]))
    put("r_b", _tiles(x["gate_r_b"][0]))
    put("i_b", _tiles(x["gate_i_b"][0]))
    put("lam", _tiles(x["lru_lambda"][0]))
    put("router", x["router_w"][0].reshape(KD, 128, NE).transpose(1, 0, 2).reshape(128, -1))

    band = np.zeros((128, len(BAND_TILES) * 128), np.float32)
    full = []
    for name in ("gate_r_w", "gate_i_w"):
        w = np.zeros((LRU, LRU), np.float32)
        for b in range(LRU // LRU_BLOCK):
            s = slice(LRU_BLOCK * b, LRU_BLOCK * (b + 1))
            w[s, s] = x[name][0, b]
        full.append(w)
    for n, (m, g, i) in enumerate(BAND_TILES):
        band[:, 128 * n:128 * n + 128] = full[g][128 * i:128 * i + 128, 128 * m:128 * m + 128]

    arrays = {"h_t": np.ascontiguousarray(tokens.T.reshape(KD, 128, T).transpose(1, 0, 2).reshape(128, KD * T)),
              "con": shape_constants(), "vec": vecs, "band": band, "gain": x["ffn_norm_odd"]}
    for name in ("w_in_even", "w_out_even", "ffn_w_gate", "ffn_w_up", "ffn_w_down", "w_in_odd", "w_out_odd",
                 "moe_w_gate", "moe_w_up", "moe_w_down"):
        arrays[name] = np.ascontiguousarray(x[name])

    nc = _bacc.Bacc("TRN2", target_bir_lowering=False, num_devices=1, dynamic_dma_scratch_size=2048)
    a = {name: nc.dram_tensor(f"in_{name}", arr.shape, mybir.dt.from_np(arr.dtype), kind="ExternalInput").ap()
         for name, arr in arrays.items()}
    out = nc.dram_tensor("out_h", (1, SEQ, D), F32, kind="ExternalOutput").ap()
    trunk_kernel(nc, a, out)
    r = _run(nc, [{f"in_{name}": arr for name, arr in arrays.items()}], core_ids=[0])
    return r.results[0]["out_h"]
```

```python
import numpy as np
import concourse.bass as bass
from concourse import mybir
from contextlib import ExitStack

F32 = mybir.dt.float32
F32R = mybir.dt.float32r
I32 = mybir.dt.int32
ALU = mybir.AluOpType
ACT = mybir.ActivationFunctionType
AX = mybir.AxisListType

D = 1024
SEQ = 256
META = 16
T = SEQ + META
KD = D // 128
EPS = 1e-6
CONV_CH = 512
CONV_W = 31
HEADS = 8
HD = 64
CT = CONV_CH // 128
EVEN_IN = 2560
D_FF = 2688
KF = D_FF // 128
LRU = 1408
KL = LRU // 128
LRU_BLOCK = 88
LRU_CONV = 4
NE = 8
FE = 3584
STEPS = FE // 512
CHUNK = 128

VEC = {}
_at = 0
for _name, _n in (("mix_norm_even", KD), ("ffn_norm_even", KD), ("mix_norm_odd", KD), ("conv_w", CONV_W * CT),
                  ("conv_b", CT), ("ln_g", CT), ("ln_b", CT), ("q_g", 1), ("k_g", 1), ("lru_conv_w", LRU_CONV * KL),
                  ("lru_conv_b", KL), ("r_b", KL), ("i_b", KL), ("lam", KL), ("router", KD * NE)):
    VEC[_name] = (_at, _n)
    _at += _n
NVEC = _at

QSTART = (0, 128, 256)
KSTART = (0, 128, T - 128)
QCOUNT = tuple(T - q for q in QSTART)
QOFF = (0, QCOUNT[0], QCOUNT[0] + QCOUNT[1])
NS = sum(QCOUNT)
CON = {}
_at = 0
for _name, _n in (("ident", 128), ("headblk", 128), ("tri_ge", 128), ("tri_lt", 128), ("iota", 128),
                  ("mask", NS), ("negmask", NS), ("tie", NE * NE), ("erow", NE), ("zero8", NE)):
    CON[_name] = (_at, _n)
    _at += _n
NCON = _at


def shape_constants():
    c = np.zeros((128, NCON), np.float32)
    p = np.arange(128)[:, None]
    m = np.arange(128)[None, :]

    def put(name, a):
        c[:, CON[name][0]:CON[name][0] + CON[name][1]] = a

    put("ident", p == m)
    put("headblk", p // HD == m // HD)
    put("tri_ge", p >= m)
    put("tri_lt", p < m)
    put("iota", m)
    mask = np.zeros((128, NS), np.float32)
    for ch in range(3):
        key = KSTART[ch] + p
        query = np.arange(QSTART[ch], T)[None, :]
        mask[:, QOFF[ch]:QOFF[ch] + QCOUNT[ch]] = (key < query) & (key >= 128 * ch)
    put("mask", mask)
    put("negmask", -mask)
    e = np.arange(NE)
    put("tie", (e[None, :] < e[:, None]).reshape(1, -1))
    put("erow", e[None, :])
    return c


def band_inputs(m):
    return [i for i in (m - 1, m, m + 1) if 0 <= i < KL]


BAND_UNITS = [[m for m in (2 * j, 2 * j + 1) if m < KL] for j in range((KL + 1) // 2)]
BAND_TILES = [(m, g, i) for ms in BAND_UNITS for m in ms for g in range(2) for i in band_inputs(m)]


def unit_table():
    units = []
    for c in range(2):
        units.append(("w_in_even", 256 * c, KD, 256))
        units.append(("w_in_even", CONV_CH + 256 * c, KD, 256))
    for c in range(4):
        units.append(("w_in_even", 2 * CONV_CH + 256 * c, KD, 256))
    units.append(("w_v", 0, KD // 2, 512))
    units.append(("w_v", KD // 2, KD // 2, 512))
    for c in range(4):
        units.append(("w_out_even", 256 * c, KD, 256))
    for c in range((KF + 1) // 2):
        w = min(256, D_FF - 256 * c)
        units.append(("ffn_w_gate", 256 * c, KD, w))
        units.append(("ffn_w_up", 256 * c, KD, w))
    for c in range(4):
        for k0 in range(0, KF, 8):
            units.append(("ffn_w_down", (256 * c, k0), min(8, KF - k0), 256))
    for c in range((KL + 1) // 2):
        for base in (LRU, 0):
            units.append(("w_in_odd", base + 256 * c, KD, min(256, LRU - 256 * c)))
    at = 0
    for ms in BAND_UNITS:
        n = sum(2 * len(band_inputs(m)) for m in ms)
        units.append(("band", at, n, 128))
        at += n
    for k0 in range(0, KL, 2):
        units.append(("w_out_odd", k0, min(2, KL - k0), D))
    return units


UNITS = unit_table()
U_CONV, U_Q, U_K, U_V, U_OUT_E = 0, 4, 6, 8, 10
U_FFN1 = 14
U_FFN2 = U_FFN1 + 2 * ((KF + 1) // 2)
U_IN_O = U_FFN2 + 12
U_BAND = U_IN_O + 2 * ((KL + 1) // 2)
U_OUT_O = U_BAND + len(BAND_UNITS)
U_MOE = U_OUT_O + (KL + 1) // 2
assert U_MOE == len(UNITS)

PRODUCTS_PER_UNIT, CONV_PER_UNIT = 7, 7
PRODUCTS_PER_PAIR, CONV_PER_PAIR = 12, 8
PROD = 4
RAW = 7
MOE_RAW = 14
SPLIT = 3
WIDTH = 2048
PER_ITEM = 6 * STEPS
assert PER_ITEM % MOE_RAW == 0 and PER_ITEM % SPLIT == 0
MAX_EXTRA = 3
ITEMS = NE + MAX_EXTRA + 1

RECUR_SPLIT = 3
RECUR_AT = {U_BAND + 3: (0, 1), U_BAND + 4: (2, 3), U_BAND + 5: (4,), U_OUT_O: (5, 6, 7), U_OUT_O + 1: (8, 9, 10)}
assert [m for ms in RECUR_AT.values() for m in ms] == list(range(KL))


def g_unit(s):
    return 0 if s == 0 else 4 + 6 * (s - 1)


def u_unit(s):
    return g_unit(s) + 2


def d_unit(s):
    return 8 + 6 * s if s < STEPS - 1 else PER_ITEM - 2


def trunk_kernel(nc, a, out):
    base = [(nc.sbuf_base + 63) // 64 * 64]
    ctx = ExitStack()

    def sb(name, shape, dt=F32):
        n = 4
        for s in shape[1:]:
            n *= s
        t = nc.alloc_sbuf_tensor_at(name, shape, dt, offset=base[0])
        base[0] += (n + 31) // 32 * 32
        return t

    with ctx:
        raw = [sb(f"raw{i}", [128, WIDTH]) for i in range(RAW)]
        whi = [sb(f"whi{i}", [128, WIDTH], F32R) for i in range(SPLIT)]
        wlo = [sb(f"wlo{i}", [128, WIDTH], F32R) for i in range(SPLIT)]
        con = sb("con", [128, NCON])
        vec = sb("vec", [128, NVEC])
        ones = sb("ones", [128, 128])
        eps = sb("eps", [128, 1])
        top = base[0]

        h = sb("h", [128, KD, T])
        hn_top = base[0]
        hn_hi = sb("hn_hi", [128, KD, T], F32R)
        hn_lo = sb("hn_lo", [128, KD, T], F32R)
        scr = sb("scr", [128, KD, T])
        rs = sb("rs", [128, 2, T])
        phase = base[0]
        mix_hi = sb("mix_hi", [128, KD, T], F32R)
        mix_lo = sb("mix_lo", [128, KD, T], F32R)
        qf = sb("qf", [128, CT, T])
        kf = sb("kf", [128, CT, T])
        vf = sb("vf", [128, 3, 512])
        uin = sb("uin", [128, CT, T])
        cacc = sb("cacc", [128, CT, T])
        sg = sb("sg", [128, 2, T])
        prod = sb("prod", [128, PROD, T])
        zm = sb("zm", [128, 2, 2, NS])
        lx = sb("lx", [128, 2, 2, NS])
        ll = sb("ll", [128, 2, 2, NS])
        ww = sb("ww", [128, 2, 2, NS])
        e_end = base[0]
        base[0] = phase
        hid_hi = sb("hid_hi", [128, KF, T], F32R)
        hid_lo = sb("hid_lo", [128, KF, T], F32R)
        fsg = sb("fsg", [128, 2, T])
        fh = sb("fh", [128, 2, T])
        f_end = base[0]
        base[0] = phase
        xb_hi = sb("xb_hi", [128, KL, T], F32R)
        xb_lo = sb("xb_lo", [128, KL, T], F32R)
        over_xb = base[0]
        gg = sb("gg", [128, KL, SEQ])
        rg = sb("rg", [128, KL, T])
        ig = sb("ig", [128, KL, T])
        xbf = sb("xbf", [128, 2, T])
        c4 = sb("c4", [128, KL])
        c8n = sb("c8n", [128, KL])
        sp_t = sb("sp_t", [128, 4, KL])
        o_end = base[0]
        base[0] = hn_top
        tt = sb("tt", [128, KL, T])
        tt_end = base[0]
        base[0] = hn_top + 2 * 4 * KD * T
        h_tok = sb("h_tok", [128, 2, D])
        base[0] = top + 4 * KD * T
        acc = sb("acc", [128, 2, D])
        sel_m = sb("sel_m", [128, 2, CHUNK])
        sel_t = sb("sel_t", [128, 2 * CHUNK])
        cmpa = sb("cmpa", [128, 2 * NE, NE])
        cmpb = sb("cmpb", [128, 2 * NE, NE])
        assert base[0] <= tt_end
        base[0] = tt_end
        gain = sb("gain", [128, D])
        assert base[0] <= hn_top + 2 * 4 * KD * T
        xs = sb("xs", [128, 2, D])
        xe_hi = sb("xe_hi", [128, KD, CHUNK], F32R)
        xe_lo = sb("xe_lo", [128, KD, CHUNK], F32R)
        turn_top = base[0]
        ht_hi = sb("ht_hi", [128, 2, 512], F32R)
        ht_lo = sb("ht_lo", [128, 2, 512], F32R)
        row_top = base[0]
        ys = sb("ys", [128, D])
        st = sb("st", [128, 16])
        lg = sb("lg", [128, 2, NE])
        rank = sb("rank", [128, 2, NE])
        chosen = sb("chosen", [128, 2, NE])
        ex = sb("ex", [128, 2, NE])
        gates = sb("gates", [128, 2, NE])
        pos = sb("pos", [128, 2, NE])
        count = sb("count", [128, NE])
        over = sb("over", [128, NE])
        cum = sb("cum", [128, NE])
        pick = sb("pick", [128, MAX_EXTRA + 1, NE])
        tmp8 = sb("tmp8", [128, 2, NE])
        item_pos = sb("item_pos", [128, 2, ITEMS])
        item_gate = sb("item_gate", [128, 2, ITEMS])
        head_f = sb("head_f", [1, 8])
        head_i = sb("head_i", [1, 8], I32)
        m_end = base[0]
        base[0] = turn_top
        xnt = sb("xnt", [128, KD, SEQ])
        assert base[0] <= row_top
        base[0] = row_top
        sq = sb("sq", [128, D])
        base[0] = top
        silu = sb("silu", [128, 2, 512])
        hb = sb("hb", [128, 2, 512])
        assert base[0] <= hn_top
        base[0] = nc.sbuf_usable_end // 32 * 32 - 7 * 4 * WIDTH
        assert m_end <= base[0] and over_xb <= base[0] + 4 * WIDTH, (m_end, over_xb, base[0])
        over_xb_raw = sb("over_xb_raw", [128, WIDTH])
        over_gates_raw = [sb(f"over_gates_raw{i}", [128, WIDTH]) for i in range(6)]
        moe_raw = over_gates_raw + [raw[(U_MOE + j) % RAW] for j in range(RAW)] + [over_xb_raw]
        assert max(e_end, f_end, o_end) <= nc.sbuf_usable_end, (top, e_end, f_end, o_end, m_end)

        P = ctx.enter_context(nc.psum_tensor("P", [128, 8, 512], F32))

        def cst(name):
            o, n = CON[name]
            return con[:, o:o + n]

        def v(name, i=0, n=1):
            o = VEC[name][0] + i
            return vec[:, o:o + n]

        def sem(name):
            return ctx.enter_context(nc.semaphore(name))

        params_in = sem("params_in")
        h_in = [sem(f"h_in{c}") for c in range(2)]
        con_in = sem("con_in")
        ones_set = sem("ones_set")
        gain_in = sem("gain_in")
        raw_full = [sem(f"raw_full{i}") for i in range(RAW)]
        moe_full = [sem(f"moe_full{i}") for i in range(MOE_RAW)]
        turned_h, h_tok_ready = sem("turned_h"), sem("h_tok_ready")
        hi_ready = sem("hi_ready")
        lo_ready = sem("lo_ready")
        unit_used = sem("unit_used")
        sq_ready, ss_ready, root_ready, nf_ready, nhi_ready, norm_ready = (
            sem(n) for n in ("sq_ready", "ss_ready", "root_ready", "nf_ready", "nhi_ready", "norm_ready"))
        dve_step = sem("dve_step")
        act_step = sem("act_step")
        sig_ready = sem("sig_ready")
        uin_ready = sem("uin_ready")
        conv_step = sem("conv_step")
        prod_ready = sem("prod_ready")
        pool_conv = sem("pool_conv")
        qk_copied = sem("qk_copied")
        qk_squared = sem("qk_squared")
        v_copied = sem("v_copied")
        qk_ss, qk_root, qk_normed = (sem(n) for n in ("qk_ss", "qk_root", "qk_normed"))
        z_done, zm_ready, ln_ready, l_ready, r_done, wz_ready, wexp_ready, w_ready, pv_done = (
            sem(n) for n in ("z_done", "zm_ready", "ln_ready", "l_ready", "r_done", "wz_ready", "wexp_ready",
                             "w_ready", "pv_done"))
        attn_hi, attn_lo = sem("attn_hi"), sem("attn_lo")
        mean_done, xc_ready, xsq_ready, var_done, var_root, ln_scaled, ln_silu, ln_hi, ln_lo = (
            sem(n) for n in ("mean_done", "xc_ready", "xsq_ready", "var_done", "var_root", "ln_scaled",
                             "ln_silu", "ln_hi", "ln_lo"))
        added_e = sem("added_e")
        ffn_silu, ffn_h, ffn_hi, ffn_lo, added_f = (sem(n) for n in ("ffn_silu", "ffn_h", "ffn_hi", "ffn_lo", "added_f"))
        xb_ready, xb_hi_ready, xb_lo_ready, gelu_ready, gates_ready = (
            sem(n) for n in ("xb_ready", "xb_hi_ready", "xb_lo_ready", "gelu_ready", "gates_ready"))
        lam_exp, lam_ready = sem("lam_exp"), sem("lam_ready")
        tanh_ready, decay_ready, bscale_ready, xi_sum, xi_ready = (
            sem(n) for n in ("tanh_ready", "decay_ready", "bscale_ready", "xi_sum", "xi_ready"))
        y_ready, y_hi_ready, y_lo_ready = sem("y_ready"), sem("y_hi_ready"), sem("y_lo_ready")
        h2_ready, h2_sq, h2_inv, h2_root, xs_ready = (
            sem(n) for n in ("h2_ready", "h2_sq", "h2_inv", "h2_root", "xs_ready"))
        xt_done, xt_copied, logits_done, lmax_ready, lexp_ready, chosen_ready, slots_done, items_ready, head_ready = (
            sem(n) for n in ("xt_done", "xt_copied", "logits_done", "lmax_ready", "lexp_ready", "chosen_ready",
                             "slots_done", "items_ready", "head_ready"))
        sel_ready, gathered, xe_hi_ready, xe_ready = (sem(n) for n in ("sel_ready", "gathered", "xe_hi_ready", "xe_ready"))
        selt_done, selt_ready = sem("selt_done"), sem("selt_ready")
        silu_ready, h_ready, turned, ht_hi_ready, ht_ready = (
            sem(n) for n in ("silu_ready", "h_ready", "turned", "ht_hi_ready", "ht_ready"))
        ys_act, ys_dve, scattered, acc_added = (sem(n) for n in ("ys_act", "ys_dve", "scattered", "acc_added"))
        stored = sem("stored")

        def km(ap):
            return ap.rearrange("(k p) m -> p k m", p=128)

        view = {"w_in_even": km(a["w_in_even"][0]), "w_v": km(a["w_in_even"][0])[:, :, 2 * CONV_CH + 1024:EVEN_IN],
                "w_out_even": km(a["w_out_even"][0]), "ffn_w_gate": km(a["ffn_w_gate"][0]),
                "ffn_w_up": km(a["ffn_w_up"][0]), "ffn_w_down": km(a["ffn_w_down"][0]),
                "w_in_odd": km(a["w_in_odd"][0]), "w_out_odd": km(a["w_out_odd"][0])}

        def unit_source(u):
            name, at, k, w = UNITS[u]
            if name == "band":
                return a["band"][:, at * 128:(at + k) * 128].rearrange("p (k m) -> p k m", m=128)
            if name in ("w_v", "w_out_odd"):
                return view[name][:, at:at + k, :]
            if name == "ffn_w_down":
                return view[name][:, at[1]:at[1] + k, at[0]:at[0] + w]
            return view[name][:, 0:k, at:at + w]

        def unit_width(u):
            return UNITS[u][2] * UNITS[u][3]

        def pair(u):
            return 2 * (u % 3)

        def both(x):
            return x.unsqueeze(1).to_broadcast([128, 2, NS])

        def band_bank(j):
            return 4 * ((j + 1) % 2)

        def turn_bank(s):
            return 1 if s == STEPS - 1 else 6 + s % 2

        def scatter_bank(n):
            return (6, 7, 4, 5)[n]

        block = ctx.enter_context(nc.Block())

        @block.sync
        def _(sp):
            h_t = a["h_t"].rearrange("p (k t) -> p k t", k=KD)
            for c in range(2):
                sp.dma_start(h[:, 4 * c:4 * c + 4], h_t[:, 4 * c:4 * c + 4]).then_inc(h_in[c], 16)
            sp.dma_start(vec[:, :], a["vec"]).then_inc(params_in, 16)
            for u in range(U_MOE):
                if u == 2:
                    sp.dma_start(con[:, :], a["con"]).then_inc(con_in, 16)
                if u >= RAW:
                    sp.wait_ge(lo_ready, u - RAW + 1)
                k, w = UNITS[u][2], UNITS[u][3]
                sp.dma_start(raw[u % RAW][:, 0:k * w].rearrange("p (k m) -> p k m", k=k), unit_source(u))\
                    .then_inc(raw_full[u % RAW], 16)

            sp.wait_ge(unit_used, U_BAND)
            sp.dma_start(gain[:, :], a["gain"].to_broadcast([128, D])).then_inc(gain_in, 16)

            w_gate = a["moe_w_gate"][0].rearrange("e (k p) f -> e p k f", p=128)
            w_up = a["moe_w_up"][0].rearrange("e (k p) f -> e p k f", p=128)
            w_down = a["moe_w_down"][0].rearrange("e (k p) m -> e p k m", p=128)

            def load_expert(i, e, first=False):
                def load(k, src, kk):
                    if first and k < 6:
                        sp.wait_ge(y_ready, KL)
                    elif first and k < MOE_RAW - 1:
                        sp.wait_ge(lo_ready, U_MOE + (k - 6) - RAW + 1)
                    elif first and k == MOE_RAW - 1:
                        sp.wait_ge(unit_used, U_MOE)
                    else:
                        sp.wait_ge(lo_ready, PER_ITEM * i + (U_MOE + k - MOE_RAW + 1))
                    sp.dma_start(moe_raw[k % MOE_RAW][:, :].rearrange("p (k m) -> p k m", k=kk), src)\
                        .then_inc(moe_full[k % MOE_RAW], 16)

                for s in range(STEPS + 1):
                    if s < STEPS:
                        f = slice(512 * s, 512 * s + 512)
                        for half in range(2):
                            load(g_unit(s) + half, w_gate[e, :, 4 * half:4 * half + 4, f], 4)
                        for half in range(2):
                            load(u_unit(s) + half, w_up[e, :, 4 * half:4 * half + 4, f], 4)
                    if s >= 1:
                        for half in range(2):
                            k0 = 4 * (s - 1) + 2 * half
                            load(d_unit(s - 1) + half, w_down[e, :, k0:k0 + 2, :], 2)

            load_expert(0, 0, first=True)
            with sp.Fori(1, NE) as i:
                load_expert(i, i)
            sp.wait_ge(head_ready, 1)
            extra = sp.value_load(head_i[0:1, 0:1], min_val=0, max_val=MAX_EXTRA)
            with sp.If(extra > 0):
                with sp.Fori(0, extra) as j:
                    e = sp.value_load(head_i[0:1, bass.ds(j + 1, 1)], min_val=0, max_val=NE - 1)
                    load_expert(j + NE, e)
            sp.wait_ge(acc_added, 4 * extra + 4 * NE)
            sp.dma_start(out[0].rearrange("(c p) d -> p c d", p=128), acc[:, :, :]).then_inc(stored, 16)
            sp.wait_ge(stored, 16)

        @block.gpsimd
        def _(pool):
            pool.memset(ones[:, :], 1.0).then_inc(ones_set, 1)
            pool.memset(eps[:, :], EPS).then_inc(ones_set, 1)
            pool.wait_ge(con_in, 16)

            def sums(x0, x1):
                for x in range(x0, x1):
                    n, c = x // 2 + 1, 2 + x % 2
                    pool.wait_ge(prod_ready, x + 3)
                    if x >= 2:
                        pool.wait_ge(pool_conv, x - 1)
                    pool.tensor_tensor(cacc[:, c, n:T], cacc[:, c, n:T], prod[:, x % PROD, 0:T - n], ALU.add)\
                        .then_inc(pool_conv, 1)

            made = [min(PRODUCTS_PER_UNIT * (U_OUT_E - U_Q) + PRODUCTS_PER_PAIR * p, 2 * CONV_W) - 2
                    for p in range(HEADS // 2)] + [2 * (CONV_W - 1)]
            assert made[-2] == made[-1]
            sums(0, made[0])
            for p in range(HEADS // 2):
                sums(made[p], made[p + 1])
                pool.wait_ge(wexp_ready, p + 1)
                pool.tensor_tensor(ww[:, p % 2], ww[:, p % 2], both(cst("mask")), ALU.mult).then_inc(w_ready, 1)
            for j, ms in enumerate(BAND_UNITS):
                m0, n = ms[0], len(ms)
                pool.wait_ge(xb_lo_ready, len(BAND_UNITS))
                if j >= 1:
                    pool.wait_ge(xi_ready, j)
                pool.tensor_tensor(xbf[:, 0:n], xb_hi[:, m0:m0 + n].bitcast(F32), xb_lo[:, m0:m0 + n].bitcast(F32),
                                   ALU.add).then_inc(xi_sum, 1)
                pool.wait_ge(xi_sum, j + 1)
                pool.wait_ge(gates_ready, j + 1)
                pool.tensor_tensor(ig[:, m0:m0 + n], ig[:, m0:m0 + n], xbf[:, 0:n], ALU.mult).then_inc(xi_ready, 1)

        @block.scalar
        def _(act):
            steps = [0]

            def step(ins):
                steps[0] += 1
                ins.then_inc(act_step, 1)
                act.wait_ge(act_step, steps[0])

            def split_hi(u):
                act.wait_ge(raw_full[u % RAW], 16 * (u // RAW + 1))
                if u >= SPLIT:
                    act.wait_ge(unit_used, u - SPLIT + 1)
                w = unit_width(u)
                act.activation(whi[u % SPLIT][:, 0:w], raw[u % RAW][:, 0:w], ACT.Copy).then_inc(hi_ready, 1)

            def inverse_root(dst, total, n, ready):
                step(act.activation(dst, total, ACT.Ln, scale=1.0 / n, bias=eps[:, 0:1]))
                act.activation(dst, dst, ACT.Exp, scale=-0.5).then_inc(ready, 1)

            def square_pair(n, c):
                if n > 0:
                    act.wait_ge(added_e if n == 1 else added_f, c + 1)
                act.activation(scr[:, 2 * c:2 * c + 2], h[:, 2 * c:2 * c + 2], ACT.Square).then_inc(sq_ready, 1)

            def norm_high(n):
                act.wait_ge(ss_ready, n + 1)
                inverse_root(rs[:, 0], P[:, 7, 0:T], D, root_ready)
                for c in range(4):
                    act.wait_ge(nf_ready, KD * n + 2 * c + 2)
                    act.activation(hn_hi[:, 2 * c:2 * c + 2], scr[:, 2 * c:2 * c + 2], ACT.Copy).then_inc(nhi_ready, 1)

            products_at = [0]

            def products(n):
                for x in range(products_at[0], min(products_at[0] + n, 2 * CONV_W)):
                    s, c = x // 2, 2 + x % 2
                    w = v("conv_w", (CONV_W - 1 - s) * CT + c)
                    if s == 0:
                        act.activation(cacc[:, c], uin[:, c], ACT.Identity, scale=w, bias=v("conv_b", c))\
                            .then_inc(prod_ready, 1)
                    else:
                        if x - 2 >= PROD:
                            act.wait_ge(pool_conv, x - 2 - PROD + 1)
                        act.activation(prod[:, (x - 2) % PROD, 0:T - s], uin[:, c, 0:T - s], ACT.Copy, scale=w)\
                            .then_inc(prod_ready, 1)
                products_at[0] = min(products_at[0] + n, 2 * CONV_W)

            def after(u):
                if u in (1, 3):
                    act.wait_ge(unit_used, u + 1)
                    if u == 3:
                        act.wait_ge(uin_ready, 1)
                    act.activation(sg[:, :, :], P[:, pair(u):pair(u) + 2, 0:T], ACT.Sigmoid).then_inc(sig_ready, 1)
                    if u == 3:
                        act.preload_act_table_set("natural_log_exp_and_others")
                elif U_Q <= u < U_OUT_E:
                    if u < U_V:
                        dst, c = (qf if u < U_K else kf), 2 * ((u - U_Q) % 2)
                        act.wait_ge(unit_used, u + 1)
                        act.activation(dst[:, c:c + 2], P[:, pair(u):pair(u) + 2, 0:T], ACT.Copy).then_inc(qk_copied, 1)
                        c = 2 * (u - U_Q)
                        act.activation(scr[:, c:c + 2, :], P[:, pair(u):pair(u) + 2, 0:T], ACT.Square)\
                            .then_inc(qk_squared, 1)
                    if u == U_V + 1:
                        act.wait_ge(unit_used, u + 1)
                        act.activation(vf[:, 0:2], P[:, 4:6, :], ACT.Copy)
                        act.activation(vf[:, 2], P[:, 0, :], ACT.Copy).then_inc(v_copied, 1)
                    if u >= U_K:
                        n = u - U_K
                        act.wait_ge(qk_ss, n + 1)
                        if n >= 1:
                            act.wait_ge(qk_normed, 2 * n)
                        inverse_root(rs[:, :, :], P[:, 6:8, 0:T], HD, qk_root)
                    if u == U_Q:
                        act.wait_ge(uin_ready, 2)
                        act.wait_ge(params_in, 16)
                    products(PRODUCTS_PER_UNIT)
                    if u == U_V + 1:
                        attention()
                elif U_OUT_E <= u < U_FFN1:
                    if u == U_OUT_E:
                        act.preload_act_table_set("natural_log_exp_and_others")
                    square_pair(1, u - U_OUT_E)
                    if u == U_FFN1 - 1:
                        norm_high(1)
                elif U_FFN1 <= u < U_FFN2 and (u - U_FFN1) % 2 == 1:
                    j = (u - U_FFN1) // 2
                    n = min(2, KF - 2 * j)
                    act.wait_ge(unit_used, u)
                    if j >= 1:
                        act.wait_ge(ffn_h, j)
                    act.activation(fsg[:, 0:n], P[:, pair(u - 1):pair(u - 1) + n, 0:T], ACT.Silu).then_inc(ffn_silu, 1)
                    act.wait_ge(ffn_h, j + 1)
                    act.activation(hid_hi[:, 2 * j:2 * j + n], fh[:, 0:n], ACT.Copy).then_inc(ffn_hi, 1)
                elif U_FFN2 <= u < U_IN_O and (u - U_FFN2) % 3 == 2:
                    if u == U_FFN2 + 2:
                        act.preload_act_table_set("natural_log_exp_and_others")
                    square_pair(2, (u - U_FFN2) // 3)
                    if u == U_IN_O - 1:
                        norm_high(2)
                        step(act.activation(sp_t[:, 0], v("lam", 0, KL), ACT.Abs))
                        act.activation(sp_t[:, 0], sp_t[:, 0], ACT.Exp, scale=-1.0).then_inc(lam_exp, 1)
                elif U_IN_O <= u < U_BAND:
                    if u - U_IN_O in (3, 6):
                        c = (u - U_IN_O) // 3 - 1
                        act.wait_ge(turned_h, c + 1)
                        act.activation(h_tok[:, c].rearrange("p (b n) -> p b n", b=2), P[:, 6:8, :], ACT.Copy)\
                            .then_inc(h_tok_ready, 1)
                    j = (u - U_IN_O) // 2
                    n = min(2, KL - 2 * j)
                    if (u - U_IN_O) % 2 == 0:
                        act.wait_ge(xb_ready, (j + 1) * LRU_CONV * 2 if n == 2 else KL * LRU_CONV)
                        act.activation(xb_hi[:, 2 * j:2 * j + n], xbf[:, 0:n], ACT.Copy).then_inc(xb_hi_ready, 1)
                    else:
                        act.wait_ge(unit_used, u + 1)
                        act.activation(gg[:, 2 * j:2 * j + n], P[:, pair(u):pair(u) + n, 0:SEQ], ACT.Gelu_apprx_tanh)\
                            .then_inc(gelu_ready, 1)
                elif U_BAND <= u < U_OUT_O:
                    j = u - U_BAND
                    act.wait_ge(unit_used, u + 1)
                    for n, m in enumerate(BAND_UNITS[j]):
                        b = band_bank(j) + 2 * n
                        act.activation(rg[:, m], P[:, b, 0:T], ACT.Sigmoid, bias=v("r_b", m))
                        last = act.activation(ig[:, m], P[:, b + 1, 0:T], ACT.Sigmoid, bias=v("i_b", m))
                    last.then_inc(gates_ready, 1)
                    act.wait_ge(lam_ready, 1)
                    act.wait_ge(gates_ready, j + 1)
                    for m in BAND_UNITS[j]:
                        last = act.activation(tt[:, m], rg[:, m], ACT.Tanh, scale=c4[:, m:m + 1])
                    last.then_inc(tanh_ready, 1)
                    if j == RECUR_SPLIT - 1:
                        decays(0, RECUR_SPLIT)
                if u == U_OUT_O:
                    decays(RECUR_SPLIT, len(BAND_UNITS))
                if u in RECUR_AT:
                    for m in RECUR_AT[u]:
                        y_high(m)

            def attention():
                def log_part(p):
                    b = p % 2
                    act.wait_ge(zm_ready, p + 1)
                    if p >= 2:
                        act.wait_ge(l_ready, p - 1)
                    step(act.activation(lx[:, b], zm[:, b], ACT.Abs))
                    step(act.activation(lx[:, b], lx[:, b], ACT.Exp, scale=-1.0))
                    act.activation(lx[:, b], lx[:, b], ACT.Ln, bias=1.0).then_inc(ln_ready, 1)

                def high(p):
                    act.wait_ge(pv_done, p + 1)
                    act.activation(mix_hi[:, CT + p], P[:, 6 + p % 2, 0:T], ACT.Copy).then_inc(attn_hi, 1)

                log_part(0)
                log_part(1)
                for p in range(HEADS // 2):
                    if p < HEADS // 2 - 1:
                        products(PRODUCTS_PER_PAIR)
                    else:
                        for c in range(CT):
                            act.wait_ge(xc_ready, c + 1)
                            act.activation(scr[:, c], cacc[:, c], ACT.Square).then_inc(xsq_ready, 1)
                    act.wait_ge(wz_ready, p + 1)
                    if p >= 2:
                        act.wait_ge(pv_done, p - 1)
                    act.activation(ww[:, p % 2], zm[:, p % 2], ACT.Exp).then_inc(wexp_ready, 1)
                    if p + 2 < HEADS // 2:
                        log_part(p + 2)
                    if p >= 1:
                        high(p - 1)
                act.wait_ge(var_done, 1)
                inverse_root(rs[:, 0], P[:, 1, 0:T], CONV_CH, var_root)
                for c in range(CT):
                    act.wait_ge(ln_scaled, c + 1)
                    act.activation(uin[:, c], cacc[:, c], ACT.Silu, scale=v("ln_g", c), bias=v("ln_b", c))\
                        .then_inc(ln_silu, 1)
                    act.wait_ge(ln_silu, c + 1)
                    act.activation(mix_hi[:, c], uin[:, c], ACT.Copy).then_inc(ln_hi, 1)
                high(HEADS // 2 - 1)

            def decays(j0, j1):
                act.wait_ge(tanh_ready, j1)
                for j in range(j0, j1):
                    for m in BAND_UNITS[j]:
                        act.activation(rg[:, m], rg[:, m], ACT.Exp, scale=c8n[:, m:m + 1]).then_inc(decay_ready, 1)
                for ms in BAND_UNITS[j0:j1]:
                    act.activation(tt[:, ms[0]:ms[0] + len(ms)], tt[:, ms[0]:ms[0] + len(ms)], ACT.Sqrt)\
                        .then_inc(bscale_ready, 1)

            def y_high(m):
                act.wait_ge(y_ready, m + 1)
                act.activation(xb_hi[:, m, 0:SEQ], tt[:, m, META:T], ACT.Copy).then_inc(y_hi_ready, 1)

            act.preload_act_table_set("natural_log_exp_and_others")
            act.wait_ge(ones_set, 2)
            for c in range(4):
                if c % 2 == 0:
                    act.wait_ge(h_in[c // 2], 16)
                square_pair(0, c)
            split_hi(0)
            norm_high(0)
            for u in range(U_MOE):
                if u >= 1:
                    split_hi(u)
                if u >= 2:
                    after(u - 2)

            def split_item_hi(i, k):
                u = U_MOE + k
                act.wait_ge(moe_full[k % MOE_RAW], 16 * (PER_ITEM // MOE_RAW) * i + 16 * (k // MOE_RAW + 1))
                act.wait_ge(unit_used, PER_ITEM * i + (u - SPLIT + 1))
                act.activation(whi[u % SPLIT][:, :], moe_raw[k % MOE_RAW][:, :], ACT.Copy).then_inc(hi_ready, 1)

            split_item_hi(0, 0)
            split_item_hi(0, 1)
            act.wait_ge(unit_used, U_MOE)
            for c in range(2):
                act.wait_ge(h2_ready, c + 1)
                act.activation(sq[:, :], acc[:, c], ACT.Square, accum_out=st[:, c:c + 1]).then_inc(h2_sq, 1)
                act.wait_ge(h2_sq, c + 1)
            act.wait_ge(h2_inv, 2)
            act.activation(st[:, 6:8], st[:, 4:6], ACT.Sqrt).then_inc(h2_root, 1)
            split_item_hi(0, 2)
            act.wait_ge(lmax_ready, 1)
            for c in range(2):
                act.activation(ex[:, c], lg[:, c], ACT.Exp, bias=st[:, 8 + c:9 + c]).then_inc(lexp_ready, 1)

            def xe_high(n):
                act.wait_ge(gathered, n + 1)
                for b in range(2):
                    last = act.activation(xe_hi[:, 4 * b:4 * b + 4], P[:, 6 + b, :].rearrange("p (k t) -> p k t", k=4),
                                          ACT.Copy)
                last.then_inc(xe_hi_ready, 1)

            xe_high(0)

            def finish(i):
                act.wait_ge(unit_used, PER_ITEM * i + (U_MOE + PER_ITEM))
                act.activation(ys[:, 0:512], P[:, 4, :], ACT.Copy).then_inc(ys_act, 1)

            def item(i, first):
                for k in range(PER_ITEM):
                    if not (first and k < 3):
                        split_item_hi(i, k)
                    if k == 1 and not first:
                        finish(i - 1)
                    done = k - 2
                    for s in range(STEPS):
                        if done == g_unit(s) + 1:
                            if s >= 1:
                                turn_high(i, s - 1)
                            act.wait_ge(unit_used, PER_ITEM * i + (U_MOE + done + 1))
                            if s >= 2:
                                act.wait_ge(h_ready, STEPS * i + (s - 1))
                            act.activation(silu[:, s % 2], P[:, s % 2, :], ACT.Silu).then_inc(silu_ready, 1)
                    if done == u_unit(0) + 1:
                        act.wait_ge(selt_done, i + 1)
                        act.activation(sel_t[:, :], P[:, 7, 0:2 * CHUNK], ACT.Copy).then_inc(selt_ready, 1)
                    if done == d_unit(STEPS - 2) + 1:
                        turn_high(i, STEPS - 1)
                        xe_high(i + 1)

            def turn_high(i, s):
                act.wait_ge(turned, STEPS * i + (s + 1))
                if s >= 2:
                    act.wait_ge(unit_used, PER_ITEM * i + (U_MOE + d_unit(s - 2) + 2))
                act.activation(ht_hi[:, s % 2], P[:, turn_bank(s), :], ACT.Copy).then_inc(ht_hi_ready, 1)

            item(0, True)
            with act.Fori(1, NE) as i:
                item(i, False)
            act.wait_ge(head_ready, 1)
            extra = act.value_load(head_i[0:1, 0:1], min_val=0, max_val=MAX_EXTRA)
            with act.If(extra > 0):
                with act.Fori(NE, extra + NE) as i:
                    item(i, False)
            finish(extra + (NE - 1))

        @block.vector
        def _(dve):
            steps = [0]

            def step(ins):
                steps[0] += 1
                ins.then_inc(dve_step, 1)
                dve.wait_ge(dve_step, steps[0])

            def split_lo(u):
                dve.wait_ge(hi_ready, u + 1)
                w = unit_width(u)
                dve.tensor_tensor(wlo[u % SPLIT][:, 0:w], raw[u % RAW][:, 0:w], whi[u % SPLIT][:, 0:w].bitcast(F32),
                                  ALU.subtract).then_inc(lo_ready, 1)

            def inverse(dst, src, n, ready, at):
                dve.tensor_scalar(dst, src, 1.0 / n, EPS, ALU.mult, ALU.add).then_inc(ready, 1)
                dve.wait_ge(ready, at + 1)
                dve.reciprocal(dst, dst).then_inc(ready, 1)

            def norm_low(n):
                g = ("mix_norm_even", "ffn_norm_even", "mix_norm_odd")[n]
                dve.wait_ge(root_ready, n + 1)
                for c in range(5):
                    if c < 4:
                        for k in (2 * c, 2 * c + 1):
                            dve.scalar_tensor_tensor(out=scr[:, k], in0=h[:, k], scalar=v(g, k), in1=rs[:, 0],
                                                     op0=ALU.mult, op1=ALU.mult).then_inc(nf_ready, 1)
                    if c >= 1:
                        p = slice(2 * c - 2, 2 * c)
                        dve.wait_ge(nf_ready, KD * n + 2 * c)
                        dve.wait_ge(nhi_ready, 4 * n + c)
                        dve.tensor_tensor(hn_lo[:, p], scr[:, p], hn_hi[:, p].bitcast(F32), ALU.subtract)\
                            .then_inc(norm_ready, 1)

            conv_at = [0]

            def conv(n):
                for x in range(conv_at[0], min(conv_at[0] + n, 2 * CONV_W)):
                    s, c = x // 2, x % 2
                    w = v("conv_w", (CONV_W - 1 - s) * CT + c)
                    if s == 0:
                        dve.tensor_scalar(cacc[:, c], uin[:, c], w, v("conv_b", c), ALU.mult, ALU.add)\
                            .then_inc(conv_step, 1)
                    else:
                        dve.wait_ge(conv_step, x - 1)
                        dve.scalar_tensor_tensor(out=cacc[:, c, s:T], in0=uin[:, c, 0:T - s], scalar=w,
                                                 in1=cacc[:, c, s:T], op0=ALU.mult, op1=ALU.add).then_inc(conv_step, 1)
                conv_at[0] = min(conv_at[0] + n, 2 * CONV_W)

            def after(u):
                if u in (1, 3):
                    c = u // 2
                    dve.wait_ge(sig_ready, c + 1)
                    dve.tensor_tensor(uin[:, 2 * c:2 * c + 2], P[:, pair(u - 1):pair(u - 1) + 2, 0:T], sg[:, :, :],
                                      ALU.mult).then_inc(uin_ready, 1)
                    if u == 3:
                        dve.wait_ge(uin_ready, 2)
                elif U_Q <= u < U_OUT_E:
                    if u >= U_K:
                        qk_norm(u - U_K)
                    conv(CONV_PER_UNIT)
                    if u == U_V + 1:
                        attention()
                elif U_OUT_E <= u < U_FFN1:
                    m = 2 * (u - U_OUT_E)
                    dve.wait_ge(unit_used, u + 1)
                    dve.tensor_tensor(h[:, m:m + 2], P[:, pair(u):pair(u) + 2, 0:T], h[:, m:m + 2], ALU.add)\
                        .then_inc(added_e, 1)
                    if u == U_FFN1 - 1:
                        dve.wait_ge(added_e, 4)
                        norm_low(1)
                elif U_FFN1 <= u < U_FFN2 and (u - U_FFN1) % 2 == 1:
                    j = (u - U_FFN1) // 2
                    n = min(2, KF - 2 * j)
                    dve.wait_ge(unit_used, u + 1)
                    dve.wait_ge(ffn_silu, j + 1)
                    if j >= 1:
                        dve.wait_ge(ffn_lo, j)
                    dve.tensor_tensor(fh[:, 0:n], fsg[:, 0:n], P[:, pair(u):pair(u) + n, 0:T], ALU.mult)\
                        .then_inc(ffn_h, 1)
                    dve.wait_ge(ffn_h, j + 1)
                    dve.wait_ge(ffn_hi, j + 1)
                    dve.tensor_tensor(hid_lo[:, 2 * j:2 * j + n], fh[:, 0:n],
                                      hid_hi[:, 2 * j:2 * j + n].bitcast(F32), ALU.subtract).then_inc(ffn_lo, 1)
                elif U_FFN2 <= u < U_IN_O and (u - U_FFN2) % 3 == 2:
                    c = (u - U_FFN2) // 3
                    b = 2 * (c % 3)
                    dve.wait_ge(unit_used, u + 1)
                    dve.tensor_tensor(h[:, 2 * c:2 * c + 2], P[:, b:b + 2, 0:T], h[:, 2 * c:2 * c + 2], ALU.add)\
                        .then_inc(added_f, 1)
                    if c == 3:
                        dve.wait_ge(added_f, 4)
                        norm_low(2)
                        decay_rates()
                elif U_IN_O <= u < U_BAND and (u - U_IN_O) % 2 == 0:
                    lru_conv(u)
                elif u in RECUR_AT:
                    recurrence(RECUR_AT[u])

            def qk_norm(n):
                x, g = (qf, "q_g") if n < 2 else (kf, "k_g")
                dve.wait_ge(qk_root, n + 1)
                for c in range(2):
                    j = 2 * (n % 2) + c
                    dve.scalar_tensor_tensor(out=x[:, j], in0=x[:, j], scalar=v(g), in1=rs[:, c],
                                             op0=ALU.mult, op1=ALU.mult).then_inc(qk_normed, 1)

            def attention():
                dve.wait_ge(con_in, 16)

                def masked(p):
                    dve.wait_ge(z_done, p + 1)
                    if p >= 2:
                        dve.wait_ge(wexp_ready, p - 1)
                    z = 2 * (p % 2)
                    for hd in range(2):
                        ins = dve.scalar_tensor_tensor(out=zm[:, p % 2, hd], in0=P[:, z + hd, 0:NS],
                                                       scalar=HD ** -0.5, in1=cst("mask"), op0=ALU.mult, op1=ALU.mult)
                    ins.then_inc(zm_ready, 1)

                def log_not(p):
                    b = p % 2
                    dve.wait_ge(ln_ready, p + 1)
                    dve.wait_ge(zm_ready, p + 1)
                    if p >= 2:
                        dve.wait_ge(r_done, p - 1)
                    step(dve.scalar_tensor_tensor(out=ll[:, b], in0=zm[:, b], scalar=0.0, in1=lx[:, b],
                                                  op0=ALU.max, op1=ALU.add))
                    dve.tensor_tensor(ll[:, b], ll[:, b], both(cst("negmask")), ALU.mult).then_inc(l_ready, 1)

                def centre():
                    dve.wait_ge(mean_done, 1)
                    dve.wait_ge(conv_step, 2 * CONV_W)
                    dve.wait_ge(pool_conv, 2 * (CONV_W - 1))
                    for c in range(CT):
                        dve.scalar_tensor_tensor(out=cacc[:, c], in0=P[:, 0, 0:T], scalar=-1.0 / CONV_CH,
                                                 in1=cacc[:, c], op0=ALU.mult, op1=ALU.add).then_inc(xc_ready, 1)

                masked(0)
                masked(1)
                conv(CONV_PER_PAIR)
                log_not(0)
                for p in range(HEADS // 2):
                    if p + 1 < HEADS // 2:
                        log_not(p + 1)
                    if p < HEADS // 2 - 1:
                        conv(CONV_PER_PAIR)
                    else:
                        centre()
                    dve.wait_ge(r_done, p + 1)
                    dve.tensor_tensor(zm[:, p % 2], P[:, 4:6, 0:NS], zm[:, p % 2], ALU.add).then_inc(wz_ready, 1)
                    if p + 2 < HEADS // 2:
                        masked(p + 2)
                    if p >= 1:
                        attn_low(p - 1)
                dve.wait_ge(var_root, 1)
                dve.wait_ge(xc_ready, CT)
                for c in range(CT + 1):
                    if c < CT:
                        dve.tensor_tensor(cacc[:, c], cacc[:, c], rs[:, 0], ALU.mult).then_inc(ln_scaled, 1)
                    if c >= 1:
                        dve.wait_ge(ln_hi, c)
                        dve.tensor_tensor(mix_lo[:, c - 1], uin[:, c - 1], mix_hi[:, c - 1].bitcast(F32),
                                          ALU.subtract).then_inc(ln_lo, 1)
                attn_low(HEADS // 2 - 1)

            def attn_low(j):
                dve.wait_ge(attn_hi, j + 1)
                dve.tensor_tensor(mix_lo[:, CT + j], P[:, 6 + j % 2, 0:T], mix_hi[:, CT + j].bitcast(F32),
                                  ALU.subtract).then_inc(attn_lo, 1)

            def decay_rates():
                x, s, s2, q = (sp_t[:, n] for n in range(4))
                dve.wait_ge(lam_exp, 1)
                step(dve.tensor_scalar(s, x, 2.0, None, ALU.add))
                step(dve.reciprocal(s, s))
                step(dve.tensor_tensor(s, s, x, ALU.mult))
                step(dve.tensor_tensor(s2, s, s, ALU.mult))
                terms = range(19, 1, -2)
                step(dve.tensor_scalar(q, s2, 1.0 / 21, 1.0 / 19, ALU.mult, ALU.add))
                for n in terms:
                    if n == 19:
                        continue
                    step(dve.tensor_tensor(q, q, s2, ALU.mult))
                    step(dve.tensor_scalar(q, q, 1.0 / n, None, ALU.add))
                step(dve.tensor_tensor(q, q, s2, ALU.mult))
                step(dve.tensor_scalar(q, q, 1.0, 8.0, ALU.add, ALU.mult))
                step(dve.tensor_tensor(q, q, s, ALU.mult))
                step(dve.tensor_scalar(s2, v("lam", 0, KL), -4.0, 0.0, ALU.mult, ALU.max))
                step(dve.tensor_tensor(c4[:, :], q, s2, ALU.add))
                dve.tensor_scalar(c8n[:, :], c4[:, :], -2.0, None, ALU.mult).then_inc(lam_ready, 1)

            def lru_conv(u):
                j = (u - U_IN_O) // 2
                n = min(2, KL - 2 * j)
                dve.wait_ge(unit_used, u + 1)
                if j >= 1:
                    dve.wait_ge(xb_lo_ready, j)
                for s in range(LRU_CONV):
                    for t in range(n):
                        m = 2 * j + t
                        w = v("lru_conv_w", (LRU_CONV - 1 - s) * KL + m)
                        x = P[:, pair(u) + t, 0:T - s]
                        if s == 0:
                            ins = dve.tensor_scalar(xbf[:, t], x, w, v("lru_conv_b", m), ALU.mult, ALU.add)
                        else:
                            dve.wait_ge(xb_ready, 2 * LRU_CONV * j + n * (s - 1) + t + 1)
                            ins = dve.scalar_tensor_tensor(out=xbf[:, t, s:T], in0=x, scalar=w, in1=xbf[:, t, s:T],
                                                           op0=ALU.mult, op1=ALU.add)
                        ins.then_inc(xb_ready, 1)
                dve.wait_ge(xb_ready, 2 * LRU_CONV * j + LRU_CONV * n)
                dve.wait_ge(xb_hi_ready, j + 1)
                dve.tensor_tensor(xb_lo[:, 2 * j:2 * j + n], xbf[:, 0:n], xb_hi[:, 2 * j:2 * j + n].bitcast(F32),
                                  ALU.subtract).then_inc(xb_lo_ready, 1)

            def recurrence(tiles):
                for m in tiles:
                    dve.wait_ge(xi_ready, m // 2 + 1)
                    dve.wait_ge(decay_ready, m + 1)
                    dve.wait_ge(bscale_ready, m // 2 + 1)
                    step(dve.scalar_tensor_tensor(out=tt[:, m], in0=rg[:, m], scalar=1.0, in1=tt[:, m],
                                                  op0=ALU.add, op1=ALU.mult))
                    step(dve.tensor_tensor(ig[:, m], ig[:, m], tt[:, m], ALU.mult))
                    step(dve.tensor_tensor_scan(tt[:, m], rg[:, m], ig[:, m], 0.0, ALU.mult, ALU.add))
                    if m == 0:
                        dve.wait_ge(gelu_ready, (KL + 1) // 2)
                    dve.tensor_tensor(tt[:, m, META:T], tt[:, m, META:T], gg[:, m], ALU.mult).then_inc(y_ready, 1)
                    if m >= 1:
                        y_low(m - 1)
                if KL - 1 in tiles:
                    y_low(KL - 1)

            def y_low(m):
                dve.wait_ge(y_hi_ready, m + 1)
                dve.tensor_tensor(xb_lo[:, m, 0:SEQ], tt[:, m, META:T], xb_hi[:, m, 0:SEQ].bitcast(F32),
                                  ALU.subtract).then_inc(y_lo_ready, 1)

            dve.wait_ge(params_in, 16)
            split_lo(0)
            norm_low(0)
            for u in range(U_MOE):
                if u >= 1:
                    split_lo(u)
                if u >= 2:
                    after(u - 2)

            def split_item_lo(i, k):
                u = U_MOE + k
                dve.wait_ge(hi_ready, PER_ITEM * i + (u + 1))
                dve.tensor_tensor(wlo[u % SPLIT][:, :], moe_raw[k % MOE_RAW][:, :], whi[u % SPLIT][:, :].bitcast(F32),
                                  ALU.subtract).then_inc(lo_ready, 1)

            split_item_lo(0, 0)
            dve.wait_ge(unit_used, U_MOE)
            dve.wait_ge(h_tok_ready, 2)
            for c in range(2):
                dve.tensor_tensor(acc[:, c].rearrange("p (b n) -> p b n", b=2), P[:, 4 + 2 * c:6 + 2 * c, :],
                                  h_tok[:, c].rearrange("p (b n) -> p b n", b=2), ALU.add).then_inc(h2_ready, 1)
            dve.wait_ge(h2_sq, 2)
            inverse(st[:, 4:6], st[:, 0:2], D, h2_inv, 0)
            dve.wait_ge(h2_root, 1)
            dve.wait_ge(h2_ready, 2)
            dve.wait_ge(gain_in, 16)
            for c in range(2):
                dve.scalar_tensor_tensor(out=xs[:, c], in0=acc[:, c], scalar=st[:, 6 + c:7 + c], in1=gain[:, :],
                                         op0=ALU.mult, op1=ALU.mult).then_inc(xs_ready, 1)
            split_item_lo(0, 1)
            for b in range(4):
                dve.wait_ge(xt_done, b + 1)
                dve.tensor_copy(xnt[:, 2 * b:2 * b + 2], P[:, 4 + b, :].rearrange("p (k t) -> p k t", k=2))\
                    .then_inc(xt_copied, 1)
            split_item_lo(0, 2)
            dve.wait_ge(logits_done, 1)
            step(dve.tensor_copy(lg[:, :, :], P[:, 0, 0:2 * NE].rearrange("p (c e) -> p c e", c=2)))
            step(dve.tensor_reduce(st[:, 10:12], lg[:, :, :], AX.X, ALU.max))
            dve.tensor_scalar(st[:, 8:10], st[:, 10:12], -1.0, None, ALU.mult).then_inc(lmax_ready, 1)
            flat = lg[:, :, :].rearrange("p c e -> p (c e)")
            mine = flat.unsqueeze(2).to_broadcast([128, 2 * NE, NE])
            for c in range(2):
                other = lg[:, c].unsqueeze(1).to_broadcast([128, NE, NE])
                own = mine[:, NE * c:NE * c + NE]
                dve.tensor_tensor(cmpa[:, NE * c:NE * c + NE], other, own, ALU.is_gt)
                last = dve.tensor_tensor(cmpb[:, NE * c:NE * c + NE], other, own, ALU.is_equal)
            step(last)
            tie = cst("tie").rearrange("p (e j) -> p e j", e=NE)
            for c in range(2):
                last = dve.tensor_tensor(cmpb[:, NE * c:NE * c + NE], cmpb[:, NE * c:NE * c + NE], tie, ALU.mult)
            step(last)
            step(dve.tensor_tensor(cmpa[:, :, :], cmpa[:, :, :], cmpb[:, :, :], ALU.add))
            step(dve.tensor_reduce(rank[:, :, :].rearrange("p c e -> p (c e)"), cmpa[:, :, :], AX.X, ALU.add))
            dve.tensor_scalar(chosen[:, :, :], rank[:, :, :], 1.5, None, ALU.is_lt).then_inc(chosen_ready, 1)
            dve.wait_ge(chosen_ready, 1)
            dve.wait_ge(slots_done, 1)
            step(dve.scalar_tensor_tensor(out=pos[:, :, :], in0=P[:, 1, 0:2 * NE].rearrange("p (c e) -> p c e", c=2),
                                          scalar=1.0, in1=chosen[:, :, :], op0=ALU.add, op1=ALU.mult))
            step(dve.tensor_scalar(pos[:, :, :], pos[:, :, :], -1.0, None, ALU.add))
            step(dve.tensor_copy(count[:, :], P[:, 1, 2 * NE:3 * NE]))
            dve.tensor_copy(item_pos[:, :, 0:NE], pos[:, :, :]).then_inc(items_ready, 1)
            dve.wait_ge(items_ready, 1)

            def gate_table():
                dve.wait_ge(lexp_ready, 2)
                step(dve.tensor_tensor(ex[:, :, :], ex[:, :, :], chosen[:, :, :], ALU.mult))
                step(dve.tensor_reduce(st[:, 12:14], ex[:, :, :], AX.X, ALU.add))
                step(dve.reciprocal(st[:, 14:16], st[:, 12:14]))
                for c in range(2):
                    last = dve.tensor_scalar(gates[:, c], ex[:, c], st[:, 14 + c:15 + c], None, ALU.mult)
                step(last)
                step(dve.tensor_copy(item_gate[:, :, 0:NE], gates[:, :, :]))

            def further_chunks():
                step(dve.tensor_scalar(over[:, :], count[:, :], CHUNK + 0.5, None, ALU.is_gt))
                step(dve.tensor_tensor_scan(cum[:, :], over[:, :], cst("zero8"), 0.0, ALU.add, ALU.add))
                for j in range(MAX_EXTRA + 1):
                    last = dve.scalar_tensor_tensor(out=pick[:, j], in0=cum[:, :], scalar=float(j + 1), in1=over[:, :],
                                                    op0=ALU.is_equal, op1=ALU.mult)
                step(last)
                step(dve.tensor_copy(head_f[0:1, 0:1], cum[0:1, NE - 1:NE]))
                step(dve.tensor_scalar(pos[:, :, :], pos[:, :, :], -float(CHUNK), None, ALU.add))

            def further_chunk(j):
                for src, dst in ((pos, item_pos), (gates, item_gate)):
                    for c in range(2):
                        last = dve.tensor_tensor(tmp8[:, c], src[:, c], pick[:, j], ALU.mult)
                    step(last)
                    step(dve.tensor_reduce(dst[:, :, NE + j:NE + j + 1], tmp8[:, :, :], AX.X, ALU.add))
                step(dve.tensor_tensor(tmp8[:, 0], pick[:, j], cst("erow"), ALU.mult))
                step(dve.tensor_reduce(head_f[0:1, 1 + j:2 + j], tmp8[0:1, 0], AX.X, ALU.add))
                if j == MAX_EXTRA:
                    dve.tensor_copy(head_i[0:1, 0:5], head_f[0:1, 0:5]).then_inc(head_ready, 1)

            def make_sel(i):
                for c in range(2):
                    last = dve.tensor_scalar(sel_m[:, c], cst("iota"), item_pos[:, c, bass.ds(i, 1)], None,
                                             ALU.is_equal)
                last.then_inc(sel_ready, 1)

            def xe_low(n):
                dve.wait_ge(xe_hi_ready, n + 1)
                for b in range(2):
                    last = dve.tensor_tensor(xe_lo[:, 4 * b:4 * b + 4],
                                             P[:, 6 + b, :].rearrange("p (k t) -> p k t", k=4),
                                             xe_hi[:, 4 * b:4 * b + 4].bitcast(F32), ALU.subtract)
                last.then_inc(xe_ready, 1)

            make_sel(0)
            xe_low(0)

            def finish_rows(i):
                dve.wait_ge(unit_used, PER_ITEM * i + (U_MOE + PER_ITEM))
                dve.tensor_copy(ys[:, 512:D], P[:, 5, :]).then_inc(ys_dve, 1)

            def finish_add(i):
                for n in range(4):
                    c, half = n // 2, n % 2
                    part = acc[:, c, 512 * half:512 * half + 512]
                    dve.wait_ge(scattered, 4 * i + (n + 1))
                    dve.scalar_tensor_tensor(out=part, in0=P[:, scatter_bank(n), :],
                                             scalar=item_gate[:, c, bass.ds(i, 1)], in1=part,
                                             op0=ALU.mult, op1=ALU.add).then_inc(acc_added, 1)

            def turn_low(i, s):
                dve.wait_ge(ht_hi_ready, STEPS * i + (s + 1))
                dve.tensor_tensor(ht_lo[:, s % 2], P[:, turn_bank(s), :], ht_hi[:, s % 2].bitcast(F32), ALU.subtract)\
                    .then_inc(ht_ready, 1)

            def item(i, first):
                for k in range(PER_ITEM):
                    if not (first and k < 3):
                        split_item_lo(i, k)
                    if first and k == 8:
                        gate_table()
                    if first and k == 10:
                        further_chunks()
                    if first and k in (12, 14, 16, 18):
                        further_chunk((k - 12) // 2)
                    if k == 1 and not first:
                        finish_rows(i - 1)
                    done = k - 2
                    if done == g_unit(0) + 1 and not first:
                        finish_add(i - 1)
                    if done == u_unit(0) + 1 and not first:
                        dve.wait_ge(acc_added, 4 * i)
                    for s in range(STEPS):
                        if s >= 1 and done == g_unit(s) + 1:
                            turn_low(i, s - 1)
                        if done == u_unit(s) + 1:
                            dve.wait_ge(unit_used, PER_ITEM * i + (U_MOE + done + 1))
                            dve.wait_ge(silu_ready, STEPS * i + (s + 1))
                            if s >= 2:
                                dve.wait_ge(turned, STEPS * i + (s - 1))
                            dve.tensor_tensor(hb[:, s % 2], silu[:, s % 2], P[:, 2 + s % 2, :], ALU.mult)\
                                .then_inc(h_ready, 1)
                    if done == d_unit(0) + 1:
                        dve.wait_ge(selt_done, i + 1)
                        make_sel(i + 1)
                    if done == d_unit(STEPS - 2) + 1:
                        turn_low(i, STEPS - 1)
                        xe_low(i + 1)

            item(0, True)
            with dve.Fori(1, NE) as i:
                item(i, False)
            dve.wait_ge(head_ready, 1)
            extra = dve.value_load(head_i[0:1, 0:1], min_val=0, max_val=MAX_EXTRA)
            with dve.If(extra > 0):
                with dve.Fori(NE, extra + NE) as i:
                    item(i, False)
            finish_rows(extra + (NE - 1))
            dve.wait_ge(acc_added, 4 * extra + 4 * (NE - 1))
            finish_add(extra + (NE - 1))

        @block.tensor
        def _(pe):
            def three(dst, w_hi, w_lo, x_hi, x_lo, start, stop, weights_move=False):
                for n, (w, x) in enumerate(((w_hi, x_hi), (w_hi, x_lo), (w_lo, x_hi))):
                    lhs, rhs = (x, w) if weights_move else (w, x)
                    last = pe.matmul(dst, lhs, rhs, start=start and n == 0, stop=stop and n == 2)
                return last

            def features(u, x_hi, x_lo, bank, k0=0, start=True, stop=True, cols=slice(0, T), norm=None):
                k, w = UNITS[u][2], UNITS[u][3]
                pe.wait_ge(lo_ready, u + 1)
                n = cols.stop - cols.start
                for m in range(w // 128):
                    for kk in range(k):
                        at = kk * w + m * 128
                        if norm is not None and m == 0 and kk % 2 == 0:
                            pe.wait_ge(norm_ready, 4 * norm + kk // 2 + 1)
                        last = three(P[:, bank + m, 0:n], whi[u % SPLIT][:, at:at + 128], wlo[u % SPLIT][:, at:at + 128],
                                     x_hi[:, k0 + kk, cols], x_lo[:, k0 + kk, cols], start and kk == 0,
                                     stop and kk == k - 1)
                last.then_inc(unit_used, 1)

            def norm_sums(n, c):
                pe.wait_ge(sq_ready, 4 * n + c + 1)
                for k in (2 * c, 2 * c + 1):
                    last = pe.matmul(P[:, 7, 0:T], ones[:, :], scr[:, k], start=k == 0, stop=k == KD - 1)
                if c == 3:
                    last.then_inc(ss_ready, 1)

            def head_sums(n):
                pe.wait_ge(qk_squared, n + 1)
                if n == 0:
                    pe.wait_ge(con_in, 16)
                else:
                    pe.wait_ge(qk_root, n)
                for c in range(2):
                    last = pe.matmul(P[:, 6 + c, 0:T], cst("headblk"), scr[:, 2 * n + c], start=True, stop=True)
                last.then_inc(qk_ss, 1)

            pe.wait_ge(ones_set, 2)
            for c in range(4):
                norm_sums(0, c)
            for u in range(U_V):
                if u == 3 or u == 4:
                    pe.wait_ge(uin_ready, 1)
                if u == 5 or u == 6:
                    pe.wait_ge(uin_ready, 2)
                if u == 7:
                    pe.wait_ge(qk_squared, 1)
                features(u, hn_hi, hn_lo, pair(u), norm=0 if u == 0 else None)
                if u >= U_K:
                    head_sums(u - U_K)
            pe.wait_ge(qk_squared, 3)
            for u in (U_V, U_V + 1):
                pe.wait_ge(lo_ready, u + 1)
                for kk in range(4):
                    k = 4 * (u - U_V) + kk
                    for c in range(3):
                        tok = slice(KSTART[c], KSTART[c] + 128)
                        last = three(P[:, (4, 5, 0)[c], :], whi[u % SPLIT][:, 512 * kk:512 * kk + 512],
                                     wlo[u % SPLIT][:, 512 * kk:512 * kk + 512], hn_hi[:, k, tok], hn_lo[:, k, tok],
                                     k == 0, k == KD - 1, weights_move=True)
                last.then_inc(unit_used, 1)
                head_sums(u - U_K)
            pe.wait_ge(v_copied, 1)
            pe.wait_ge(qk_squared, 4)

            def scores(p):
                pe.wait_ge(qk_normed, 4 + p + 1)
                if p >= 2:
                    pe.wait_ge(zm_ready, p - 1)
                for hd in range(2):
                    r = slice(HD * hd, HD * hd + HD)
                    for c in range(3):
                        last = pe.matmul(P[:, 2 * (p % 2) + hd, QOFF[c]:QOFF[c] + QCOUNT[c]],
                                         kf[r, p, KSTART[c]:KSTART[c] + 128], qf[r, p, QSTART[c]:T],
                                         start=True, stop=True)
                last.then_inc(z_done, 1)

            def later(p):
                pe.wait_ge(l_ready, p + 1)
                if p >= 1:
                    pe.wait_ge(wz_ready, p)
                for hd in range(2):
                    for c in range(3):
                        for o in range(c, 3):
                            skip = QSTART[o] - QSTART[c]
                            last = pe.matmul(P[:, 4 + hd, QOFF[c] + skip:QOFF[c] + QCOUNT[c]],
                                             cst("tri_ge") if o == c else ones[:, :],
                                             ll[:, p % 2, hd, QOFF[o]:QOFF[o] + QCOUNT[o]], start=o == c, stop=o == 2)
                last.then_inc(r_done, 1)

            def values(p):
                pe.wait_ge(w_ready, p + 1)
                if p >= 2:
                    pe.wait_ge(attn_lo, p - 1)
                for hd in range(2):
                    r = slice(HD * hd, HD * hd + HD)
                    for c in range(3):
                        last = pe.matmul(P[r, 6 + p % 2, QSTART[c]:T], vf[:, c, HD * (2 * p + hd):HD * (2 * p + hd + 1)],
                                         ww[:, p % 2, hd, QOFF[c]:QOFF[c] + QCOUNT[c]], start=c == 0, stop=c == 2)
                last.then_inc(pv_done, 1)

            def conv_mean():
                pe.wait_ge(zm_ready, HEADS // 2 - 1)
                pe.wait_ge(conv_step, 2 * CONV_W)
                pe.wait_ge(pool_conv, 2 * (CONV_W - 1))
                for c in range(CT):
                    last = pe.matmul(P[:, 0, 0:T], ones[:, :], cacc[:, c], start=c == 0, stop=c == CT - 1)
                last.then_inc(mean_done, 1)

            def conv_variance():
                for c in range(CT):
                    pe.wait_ge(xsq_ready, c + 1)
                    last = pe.matmul(P[:, 1, 0:T], ones[:, :], scr[:, c], start=c == 0, stop=c == CT - 1)
                last.then_inc(var_done, 1)

            scores(0)
            scores(1)
            for p in range(HEADS // 2 + 1):
                if p + 2 < HEADS // 2:
                    scores(p + 2)
                if p == HEADS // 2 - 1:
                    conv_mean()
                if p < HEADS // 2:
                    later(p)
                if p == HEADS // 2 - 1:
                    conv_variance()
                if p >= 1:
                    values(p - 1)
            pe.wait_ge(ln_lo, CT)
            pe.wait_ge(attn_lo, CT)
            for u in range(U_OUT_E, U_FFN1):
                if u == U_OUT_E + 3:
                    pe.wait_ge(added_e, 1)
                features(u, mix_hi, mix_lo, pair(u))
                if u > U_OUT_E:
                    norm_sums(1, u - U_OUT_E - 1)
            norm_sums(1, 3)
            for u in range(U_FFN1, U_FFN2):
                j = (u - U_FFN1) // 2
                if u - 3 >= U_FFN1:
                    pe.wait_ge(ffn_h, (u - 3 - U_FFN1) // 2 + 1)
                features(u, hn_hi, hn_lo, pair(u), norm=1 if u == U_FFN1 else None)
            for u in range(U_FFN2, U_IN_O):
                c, part = (u - U_FFN2) // 3, (u - U_FFN2) % 3
                if u == U_FFN2:
                    pe.wait_ge(ffn_h, (KF + 1) // 2)
                if c == 0:
                    pe.wait_ge(ffn_lo, min(4 * part + 4, (KF + 1) // 2))
                if c == 3 and part == 0:
                    pe.wait_ge(added_f, 1)
                features(u, hid_hi, hid_lo, 2 * (c % 3), k0=8 * part, start=part == 0, stop=part == 2)
                if part == 0 and c >= 1:
                    norm_sums(2, c - 1)
            norm_sums(2, 3)
            def turn_residual(c):
                if c >= 1:
                    pe.wait_ge(h_tok_ready, c)
                for k in range(KD):
                    last = pe.matmul(P[:, 6 + k // 4, 128 * (k % 4):128 * (k % 4) + 128],
                                     h[:, k, META + 128 * c:META + 128 * c + 128], cst("ident"), is_transpose=True,
                                     start=True, stop=True)
                last.then_inc(turned_h, 1)

            for u in range(U_IN_O, U_BAND):
                n = u - U_IN_O
                if n in (3, 6):
                    turn_residual(n // 3 - 1)
                if n >= 3:
                    pe.wait_ge(gelu_ready if (n - 3) % 2 else xb_lo_ready, (n - 3) // 2 + 1)
                if n % 2 == 0:
                    features(u, hn_hi, hn_lo, pair(u), norm=2 if n == 0 else None)
                else:
                    features(u, hn_hi, hn_lo, pair(u), cols=slice(META, T))
            pe.wait_ge(gelu_ready, (KL + 1) // 2)
            pe.wait_ge(h_tok_ready, 2)
            for u in range(U_BAND, U_OUT_O):
                j = u - U_BAND
                pe.wait_ge(xb_lo_ready, 2 if j == 0 else (KL + 1) // 2)
                pe.wait_ge(lo_ready, u + 1)
                if j >= 2:
                    pe.wait_ge(gates_ready, j - 1)
                at = 0
                for n, m in enumerate(BAND_UNITS[j]):
                    for g in range(2):
                        near = band_inputs(m)
                        for x in near:
                            last = three(P[:, band_bank(j) + 2 * n + g, 0:T], whi[u % SPLIT][:, at:at + 128],
                                         wlo[u % SPLIT][:, at:at + 128], xb_hi[:, x], xb_lo[:, x],
                                         x == near[0], x == near[-1])
                            at += 128
                last.then_inc(unit_used, 1)
            pe.wait_ge(gates_ready, len(BAND_UNITS) - 1)
            for u in range(U_OUT_O, U_MOE):
                pe.wait_ge(lo_ready, u + 1)
                for kk in range(UNITS[u][2]):
                    m = 2 * (u - U_OUT_O) + kk
                    pe.wait_ge(y_lo_ready, m + 1)
                    for c in range(2):
                        for half in range(2):
                            at = D * kk + 512 * half
                            last = three(P[:, 4 + 2 * c + half, :], whi[u % SPLIT][:, at:at + 512],
                                         wlo[u % SPLIT][:, at:at + 512], xb_hi[:, m, 128 * c:128 * c + 128],
                                         xb_lo[:, m, 128 * c:128 * c + 128], m == 0, m == KL - 1, weights_move=True)
                last.then_inc(unit_used, 1)
            pe.wait_ge(xs_ready, 2)
            for b in range(4):
                for kk in range(2):
                    for c in range(2):
                        k = 2 * b + kk
                        last = pe.matmul(P[:, 4 + b, 256 * kk + 128 * c:256 * kk + 128 * c + 128],
                                         xs[:, c, 128 * k:128 * k + 128], cst("ident"), is_transpose=True,
                                         start=True, stop=True)
                last.then_inc(xt_done, 1)
            pe.wait_ge(xt_copied, 4)
            for c in range(2):
                for k in range(KD):
                    last = pe.matmul(P[:, 0, NE * c:NE * c + NE], xnt[:, k, 128 * c:128 * c + 128],
                                     v("router", NE * k, NE), start=k == 0, stop=k == KD - 1)
            last.then_inc(logits_done, 1)
            pe.wait_ge(chosen_ready, 1)
            pe.matmul(P[:, 1, 0:NE], cst("tri_lt"), chosen[:, 0], start=True, stop=True)
            pe.matmul(P[:, 1, NE:2 * NE], ones[:, :], chosen[:, 0], start=True, stop=False)
            pe.matmul(P[:, 1, NE:2 * NE], cst("tri_lt"), chosen[:, 1], start=False, stop=True)
            pe.matmul(P[:, 1, 2 * NE:3 * NE], ones[:, :], chosen[:, 0], start=True, stop=False)
            pe.matmul(P[:, 1, 2 * NE:3 * NE], ones[:, :], chosen[:, 1], start=False, stop=True)\
                .then_inc(slots_done, 1)

            def gather(i):
                pe.wait_ge(sel_ready, i + 1)
                for k in range(KD):
                    for c in range(2):
                        last = pe.matmul(P[:, 6 + k // 4, 128 * (k % 4):128 * (k % 4) + 128],
                                         xs[:, c, 128 * k:128 * k + 128], sel_m[:, c], start=c == 0, stop=c == 1)
                last.then_inc(gathered, 1)

            def in_features(i, k_unit, bank):
                for half in range(2):
                    u = U_MOE + k_unit + half
                    pe.wait_ge(lo_ready, PER_ITEM * i + (u + 1))
                    for kk in range(4):
                        k = 4 * half + kk
                        w = slice(512 * kk, 512 * kk + 512)
                        last = three(P[:, bank, :], whi[u % SPLIT][:, w], wlo[u % SPLIT][:, w], xe_hi[:, k], xe_lo[:, k],
                                     k == 0, k == KD - 1, weights_move=True)
                    last.then_inc(unit_used, 1)

            def turn(i, s):
                pe.wait_ge(h_ready, STEPS * i + (s + 1))
                if s >= 2:
                    pe.wait_ge(ht_ready, STEPS * i + (s - 1))
                for n in range(4):
                    last = pe.matmul(P[:, turn_bank(s), 128 * n:128 * n + 128], hb[:, s % 2, 128 * n:128 * n + 128],
                                     cst("ident"), is_transpose=True, start=True, stop=True)
                last.then_inc(turned, 1)

            def down(i, s):
                pe.wait_ge(ht_ready, STEPS * i + (s + 1))
                for half in range(2):
                    u = U_MOE + d_unit(s) + half
                    pe.wait_ge(lo_ready, PER_ITEM * i + (u + 1))
                    for kk in range(2):
                        n = 2 * half + kk
                        for o in range(2):
                            at = D * kk + 512 * o
                            last = three(P[:, 4 + o, :], whi[u % SPLIT][:, at:at + 512], wlo[u % SPLIT][:, at:at + 512],
                                         ht_hi[:, s % 2, 128 * n:128 * n + 128], ht_lo[:, s % 2, 128 * n:128 * n + 128],
                                         s == 0 and n == 0, s == STEPS - 1 and n == 3, weights_move=True)
                    last.then_inc(unit_used, 1)

            def scatter(i):
                pe.wait_ge(ys_act, i + 1)
                pe.wait_ge(ys_dve, i + 1)
                for n in range(4):
                    c, half = n // 2, n % 2
                    pe.matmul(P[:, scatter_bank(n), :], sel_t[:, 128 * c:128 * c + 128],
                              ys[:, 512 * half:512 * half + 512], start=True, stop=True).then_inc(scattered, 1)

            def item(i, first):
                pe.wait_ge(xe_ready, i + 1)
                for s in range(STEPS):
                    if s >= 2:
                        pe.wait_ge(h_ready, STEPS * i + (s - 1))
                    in_features(i, g_unit(s), s % 2)
                    if s == 0 and not first:
                        scatter(i - 1)
                    if s >= 1:
                        turn(i, s - 1)
                    in_features(i, u_unit(s), 2 + s % 2)
                    if s == 0:
                        if not first:
                            pe.wait_ge(acc_added, 4 * i)
                        for c in range(2):
                            last = pe.matmul(P[:, 7, 128 * c:128 * c + 128], sel_m[:, c], cst("ident"),
                                             is_transpose=True, start=True, stop=True)
                        last.then_inc(selt_done, 1)
                    if s >= 1:
                        if s == 1:
                            pe.wait_ge(selt_ready, i + 1)
                        down(i, s - 1)
                turn(i, STEPS - 1)
                pe.wait_ge(ht_ready, STEPS * i + (STEPS - 1))
                gather(i + 1)
                down(i, STEPS - 1)

            gather(0)
            item(0, True)
            with pe.Fori(1, NE) as i:
                item(i, False)
            pe.wait_ge(head_ready, 1)
            extra = pe.value_load(head_i[0:1, 0:1], min_val=0, max_val=MAX_EXTRA)
            with pe.If(extra > 0):
                with pe.Fori(NE, extra + NE) as i:
                    item(i, False)
            scatter(extra + (NE - 1))


def _tiles(x):
    return x.reshape(-1, 128).T


def kernel(**inputs):
    import concourse.bacc as _bacc
    from concourse.bass_utils import run_bass_kernel_spmd as _run

    x = {k: np.asarray(a) for k, a in inputs.items()}
    tokens = np.concatenate([x["meta_tokens"], x["x"][0]], axis=0)
    vecs = np.zeros((128, NVEC), np.float32)

    def put(name, value):
        at, n = VEC[name]
        vecs[:, at:at + n] = value

    put("mix_norm_even", _tiles(x["mix_norm_even"][0]))
    put("ffn_norm_even", _tiles(x["ffn_norm_even"][0]))
    put("mix_norm_odd", _tiles(x["mix_norm_odd"][0]))
    put("conv_w", x["conv_w"][0].reshape(CONV_W, CT, 128).transpose(2, 0, 1).reshape(128, -1))
    put("conv_b", _tiles(x["conv_b"][0]))
    put("ln_g", _tiles(x["conv_ln_g"][0]))
    put("ln_b", _tiles(x["conv_ln_b"][0]))
    put("q_g", np.concatenate([x["q_norm_g"][0]] * 2)[:, None])
    put("k_g", np.concatenate([x["k_norm_g"][0]] * 2)[:, None])
    put("lru_conv_w", x["lru_conv_w"][0].reshape(LRU_CONV, KL, 128).transpose(2, 0, 1).reshape(128, -1))
    put("lru_conv_b", _tiles(x["lru_conv_b"][0]))
    put("r_b", _tiles(x["gate_r_b"][0]))
    put("i_b", _tiles(x["gate_i_b"][0]))
    put("lam", _tiles(x["lru_lambda"][0]))
    put("router", x["router_w"][0].reshape(KD, 128, NE).transpose(1, 0, 2).reshape(128, -1))

    band = np.zeros((128, len(BAND_TILES) * 128), np.float32)
    full = []
    for name in ("gate_r_w", "gate_i_w"):
        w = np.zeros((LRU, LRU), np.float32)
        for b in range(LRU // LRU_BLOCK):
            s = slice(LRU_BLOCK * b, LRU_BLOCK * (b + 1))
            w[s, s] = x[name][0, b]
        full.append(w)
    for n, (m, g, i) in enumerate(BAND_TILES):
        band[:, 128 * n:128 * n + 128] = full[g][128 * i:128 * i + 128, 128 * m:128 * m + 128]

    arrays = {"h_t": np.ascontiguousarray(tokens.T.reshape(KD, 128, T).transpose(1, 0, 2).reshape(128, KD * T)),
              "con": shape_constants(), "vec": vecs, "band": band, "gain": x["ffn_norm_odd"]}
    for name in ("w_in_even", "w_out_even", "ffn_w_gate", "ffn_w_up", "ffn_w_down", "w_in_odd", "w_out_odd",
                 "moe_w_gate", "moe_w_up", "moe_w_down"):
        arrays[name] = np.ascontiguousarray(x[name])

    nc = _bacc.Bacc("TRN2", target_bir_lowering=False, num_devices=1, dynamic_dma_scratch_size=2048)
    a = {name: nc.dram_tensor(f"in_{name}", arr.shape, mybir.dt.from_np(arr.dtype), kind="ExternalInput").ap()
         for name, arr in arrays.items()}
    out = nc.dram_tensor("out_h", (1, SEQ, D), F32, kind="ExternalOutput").ap()
    trunk_kernel(nc, a, out)
    r = _run(nc, [{f"in_{name}": arr for name, arr in arrays.items()}], core_ids=[0])
    return r.results[0]["out_h"]
```
